# Optimizing a Trainium2 kernel written in Bass

```python
import math
import jax, jax.numpy as jnp
from jax import lax
import numpy as np

D_MODEL = 1024
BATCH = 1
SEQ = 256
DEPTH = 4

CHUNK = 64
N_MIXERS = 3
EPS = 1e-6

POOL_WINDOWS = (2, 4, 8, 16)
N_POOL_GROUPS = len(POOL_WINDOWS)
POOL_GROUP = D_MODEL // N_POOL_GROUPS

SB_HEAD_DIM = 64
SB_HEADS = D_MODEL // SB_HEAD_DIM
Q_BLOCK = 128

S5_GROUP = 16
S5_GROUPS = D_MODEL // S5_GROUP
S5_STATE = 64
S5_DT_MIN = 1e-3
S5_DT_MAX = 1e-1

MEM_LEN = 256
XA_HEADS = 4
XA_HEAD_DIM = D_MODEL // XA_HEADS

D_FF = ((8 * D_MODEL // 3 + 127) // 128) * 128
CONV_WIDTH = 3

N_POOL_LAYERS = (DEPTH + 2) // 3
N_SB_LAYERS = (DEPTH + 1) // 3
N_S5_LAYERS = DEPTH // 3


def rms_norm(x, g):
    xf = x.astype(jnp.float32)
    y = xf * lax.rsqrt(jnp.mean(xf * xf, axis=-1, keepdims=True) + EPS)
    return (y * g.astype(jnp.float32)).astype(x.dtype)

def causal_shift(x, k):
    return jnp.pad(x, ((0, 0), (k, 0), (0, 0)))[:, : x.shape[1]]

def pool_mixer(h, w, scale):
    B, S, D = h.shape
    hf = h.astype(jnp.float32)
    cs = jnp.cumsum(hf, axis=1)
    counts = jnp.arange(1, S + 1, dtype=jnp.float32)
    groups = []
    for gi, win in enumerate(POOL_WINDOWS):
        sl = slice(gi * POOL_GROUP, (gi + 1) * POOL_GROUP)
        c = cs[..., sl]
        win_sum = c - causal_shift(c, win)
        cnt = jnp.minimum(counts, float(win))[None, :, None]
        groups.append(win_sum / cnt - hf[..., sl])
    p = jnp.stack(groups, axis=2).astype(h.dtype)
    y = jnp.einsum('bsgc,gcd->bsgd', p, w).reshape(B, S, D)
    return y * scale

def stick_breaking_attention(h, w_qkv, w_o):
    B, S, D = h.shape
    qkv = (h @ w_qkv).reshape(B, S, 3, SB_HEADS, SB_HEAD_DIM)
    q, k, v = qkv[:, :, 0], qkv[:, :, 1], qkv[:, :, 2]
    scale = SB_HEAD_DIM ** -0.5
    outs = []
    for i in range(S // Q_BLOCK):
        q0 = i * Q_BLOCK
        kend = q0 + Q_BLOCK
        z = jnp.einsum('bqhd,bkhd->bhqk', q[:, q0:kend], k[:, :kend]).astype(jnp.float32) * scale
        qpos = q0 + jnp.arange(Q_BLOCK)
        kpos = jnp.arange(kend)
        mask = kpos[None, :] < qpos[:, None]
        log_one_minus = jnp.where(mask, jax.nn.log_sigmoid(-z), 0.0)
        between = lax.cumsum(log_one_minus, axis=3, reverse=True) - log_one_minus
        a = jnp.where(mask, jnp.exp(jax.nn.log_sigmoid(z) + between), 0.0)
        outs.append(jnp.einsum('bhqk,bkhd->bqhd', a.astype(v.dtype), v[:, :kend]))
    o = jnp.concatenate(outs, axis=1).reshape(B, S, D)
    return o @ w_o

def _lin_rec_combine(left, right):
    a1, b1 = left
    a2, b2 = right
    return a1 * a2, a2 * b1 + b2

def s5_mixer(h, a_re, a_im, log_dt, b_re, b_im, c_re, c_im, d, w_glu):
    B, S, D = h.shape
    f32 = jnp.float32
    u = h.astype(f32)
    lam = lax.complex(a_re.astype(f32), a_im.astype(f32))
    dt = jnp.exp(log_dt.astype(f32))[:, None]
    dt_lam = lam * dt
    a_bar = jnp.exp(dt_lam)
    b_bar = ((a_bar - 1.0) / lam)[..., None] * lax.complex(b_re.astype(f32), b_im.astype(f32))
    c_mat = lax.complex(c_re.astype(f32), c_im.astype(f32))
    steps = jnp.arange(1, CHUNK + 1, dtype=f32)
    a_pow = jnp.exp(steps[:, None, None] * dt_lam[None])
    n_chunks = S // CHUNK
    u_chunks = u.reshape(B, n_chunks, CHUNK, S5_GROUPS, S5_GROUP).transpose(1, 0, 2, 3, 4)

    def chunk_step(state, u_blk):
        bu = jnp.einsum('bcgi,gpi->bcgp', u_blk.astype(jnp.complex64), b_bar)
        a_seq = jnp.broadcast_to(a_bar, bu.shape)
        _, xs = lax.associative_scan(_lin_rec_combine, (a_seq, bu), axis=1)
        xs = xs + a_pow[None] * state[:, None]
        y = jnp.real(jnp.einsum('bcgp,gip->bcgi', xs, c_mat))
        return xs[:, -1], y

    state0 = jnp.zeros((B, S5_GROUPS, S5_STATE), jnp.complex64)
    _, ys = lax.scan(chunk_step, state0, u_chunks)
    y = ys.transpose(1, 0, 2, 3, 4).reshape(B, S, D) + d.astype(f32) * u
    y = jax.nn.gelu(y).astype(h.dtype)
    val, gate = jnp.split(y @ w_glu, 2, axis=-1)
    return val * jax.nn.sigmoid(gate)

def memory_cross_attention(h, mem_n, wq, wkv, wo):
    B, S, D = h.shape
    M = mem_n.shape[1]
    q = (h @ wq).reshape(B, S, XA_HEADS, XA_HEAD_DIM)
    kv = (mem_n @ wkv).reshape(B, M, 2, XA_HEADS, XA_HEAD_DIM)
    k, v = kv[:, :, 0], kv[:, :, 1]
    s = jnp.einsum('bshd,bmhd->bhsm', q, k).astype(jnp.float32) * (XA_HEAD_DIM ** -0.5)
    p = jax.nn.softmax(s, axis=-1).astype(v.dtype)
    o = jnp.einsum('bhsm,bmhd->bshd', p, v).reshape(B, S, D)
    return o @ wo

def conv_glu_ffn(h, w_up, conv_w, conv_b, w_down):
    u = h @ w_up
    u = sum(conv_w[CONV_WIDTH - 1 - k] * causal_shift(u, k) for k in range(CONV_WIDTH)) + conv_b
    val, gate = jnp.split(u, 2, axis=-1)
    return (jax.nn.silu(gate) * val) @ w_down

def first_inputs(seed: int = 0) -> dict:
    key = jax.random.key(seed)
    keys = iter(jax.random.split(key, 40))
    f32 = jnp.float32

    def nrm(shape, scale):
        return jax.random.normal(next(keys), shape, f32) * scale

    def gain(shape):
        return 1.0 + nrm(shape, 0.02)

    D, F = D_MODEL, D_FF
    G, P, Cg = S5_GROUPS, S5_STATE, S5_GROUP
    a_im_init = jnp.pi * jnp.arange(P, dtype=f32)
    return {
        "x": nrm((BATCH, SEQ, D), 1.0),
        "mem": nrm((BATCH, MEM_LEN, D), 1.0),
        "mix_norm_g": gain((DEPTH, D)),
        "pool_w": nrm((N_POOL_LAYERS, N_POOL_GROUPS, POOL_GROUP, POOL_GROUP), POOL_GROUP ** -0.5),
        "pool_scale": gain((N_POOL_LAYERS, D)),
        "sb_w_qkv": nrm((N_SB_LAYERS, D, 3 * D), D ** -0.5),
        "sb_w_o": nrm((N_SB_LAYERS, D, D), D ** -0.5),
        "s5_a_re": -0.5 + nrm((N_S5_LAYERS, G, P), 0.01),
        "s5_a_im": a_im_init + nrm((N_S5_LAYERS, G, P), 0.01),
        "s5_log_dt": jax.random.uniform(next(keys), (N_S5_LAYERS, G), f32,
                                        minval=math.log(S5_DT_MIN), maxval=math.log(S5_DT_MAX)),
        "s5_b_re": nrm((N_S5_LAYERS, G, P, Cg), (2 * Cg) ** -0.5),
        "s5_b_im": nrm((N_S5_LAYERS, G, P, Cg), (2 * Cg) ** -0.5),
        "s5_c_re": nrm((N_S5_LAYERS, G, Cg, P), (2 * P) ** -0.5),
        "s5_c_im": nrm((N_S5_LAYERS, G, Cg, P), (2 * P) ** -0.5),
        "s5_d": nrm((N_S5_LAYERS, D), 1.0),
        "s5_w_glu": nrm((N_S5_LAYERS, D, 2 * D), D ** -0.5),
        "xa_norm_g": gain((DEPTH, D)),
        "mem_norm_g": gain((DEPTH, D)),
        "xa_wq": nrm((DEPTH, D, D), D ** -0.5),
        "xa_wkv": nrm((DEPTH, D, 2 * D), D ** -0.5),
        "xa_wo": nrm((DEPTH, D, D), D ** -0.5),
        "ffn_norm_g": gain((DEPTH, D)),
        "ffn_w_up": nrm((DEPTH, D, 2 * F), D ** -0.5),
        "ffn_conv_w": nrm((DEPTH, CONV_WIDTH, 2 * F), CONV_WIDTH ** -0.5),
        "ffn_conv_b": nrm((DEPTH, 2 * F), 0.01),
        "ffn_w_down": nrm((DEPTH, F, D), F ** -0.5),
        "final_norm_g": gain((D,)),
    }

def first_block(x, mem, mix_norm_g, pool_w, pool_scale, sb_w_qkv, sb_w_o,
              s5_a_re, s5_a_im, s5_log_dt, s5_b_re, s5_b_im, s5_c_re, s5_c_im, s5_d, s5_w_glu,
              xa_norm_g, mem_norm_g, xa_wq, xa_wkv, xa_wo,
              ffn_norm_g, ffn_w_up, ffn_conv_w, ffn_conv_b, ffn_w_down, final_norm_g):
    h = x
    for i in range(DEPTH):
        kind = i % N_MIXERS
        j = i // N_MIXERS
        hn = rms_norm(h, mix_norm_g[i])
        if kind == 0:
            t = pool_mixer(hn, pool_w[j], pool_scale[j])
        elif kind == 1:
            t = stick_breaking_attention(hn, sb_w_qkv[j], sb_w_o[j])
        else:
            t = s5_mixer(hn, s5_a_re[j], s5_a_im[j], s5_log_dt[j], s5_b_re[j], s5_b_im[j],
                         s5_c_re[j], s5_c_im[j], s5_d[j], s5_w_glu[j])
        h = h + t.astype(h.dtype)
        m = memory_cross_attention(rms_norm(h, xa_norm_g[i]), rms_norm(mem, mem_norm_g[i]),
                                   xa_wq[i], xa_wkv[i], xa_wo[i])
        h = h + m.astype(h.dtype)
        f = conv_glu_ffn(rms_norm(h, ffn_norm_g[i]), ffn_w_up[i], ffn_conv_w[i], ffn_conv_b[i], ffn_w_down[i])
        h = h + f.astype(h.dtype)
    return rms_norm(h, final_norm_g)


DEPTH_2 = 2

HEAD_DIM = 64
N_HEADS_MOBA = 6
N_HEADS_MLA = 4
N_HEADS_FOX = 6
MOBA_BLOCK = 256
MOBA_TOPK = 3
MOBA_Q_BLOCK = 32
MLA_Q_RANK = 256
MLA_KV_RANK = 128
MLA_NOPE_DIM = 64
MLA_ROPE_DIM = 32
MLA_V_DIM = 64
MLA_QK_DIM = MLA_NOPE_DIM + MLA_ROPE_DIM
ROPE_THETA = 10000.0
T5_BUCKETS = 32
T5_MAX_DIST = 1024
D_FF_2 = 2816
NORM_EPS = 1e-6
NEG_INF = -1e30

W_MOBA = N_HEADS_MOBA * HEAD_DIM
W_MLA = N_HEADS_MLA * MLA_V_DIM
W_FOX = N_HEADS_FOX * HEAD_DIM
MIX_WIDTH = W_MOBA + W_MLA + W_FOX
PROJ_SIZES = (W_MOBA, W_MOBA, W_MOBA, MLA_Q_RANK, MLA_KV_RANK, MLA_ROPE_DIM, W_FOX, W_FOX, W_FOX, N_HEADS_FOX)
PROJ_COLS = sum(PROJ_SIZES)


def rms_norm_2(x, g):
    xf = x.astype(jnp.float32)
    y = xf * lax.rsqrt(jnp.mean(xf * xf, axis=-1, keepdims=True) + NORM_EPS)
    return (y * g.astype(jnp.float32)).astype(x.dtype)

def split_heads(t, n, d):
    b, s, _ = t.shape
    return t.reshape(b, s, n, d).transpose(0, 2, 1, 3)

def merge_heads(t):
    b, h, s, d = t.shape
    return t.transpose(0, 2, 1, 3).reshape(b, s, h * d)

def rotary(t, pos):
    half = t.shape[-1] // 2
    inv = ROPE_THETA ** (-jnp.arange(half, dtype=jnp.float32) / half)
    ang = pos.astype(jnp.float32)[:, None] * inv[None, :]
    cos, sin = jnp.cos(ang), jnp.sin(ang)
    t1 = t[..., :half].astype(jnp.float32)
    t2 = t[..., half:].astype(jnp.float32)
    return jnp.concatenate([t1 * cos - t2 * sin, t1 * sin + t2 * cos], axis=-1).astype(t.dtype)

def t5_bucket(rel):
    n = jnp.maximum(rel, 0)
    exact = T5_BUCKETS // 2
    large = exact + (jnp.log(jnp.maximum(n, 1).astype(jnp.float32) / exact)
                     / math.log(T5_MAX_DIST / exact) * (T5_BUCKETS - exact)).astype(jnp.int32)
    return jnp.where(n < exact, n, jnp.minimum(large, T5_BUCKETS - 1))

def moba_attention(q, k, v, rel_bias):
    b, h, s, dh = q.shape
    nb = -(-s // MOBA_BLOCK)
    pad = nb * MOBA_BLOCK - s
    kp = jnp.pad(k, ((0, 0), (0, 0), (0, pad), (0, 0)))
    vp = jnp.pad(v, ((0, 0), (0, 0), (0, pad), (0, 0)))
    k_blocks = kp.reshape(b, h, nb, MOBA_BLOCK, dh)
    v_blocks = vp.reshape(b, h, nb, MOBA_BLOCK, dh)
    k_mean = jnp.mean(k_blocks, axis=3)
    topk = min(MOBA_TOPK, nb)
    bias_tab = rel_bias.T
    scale = dh ** -0.5
    b_idx = jnp.arange(b)[:, None, None, None]
    h_idx = jnp.arange(h)[None, :, None, None]
    blk_pos = jnp.arange(MOBA_BLOCK)

    def chunk(c):
        q_start = c * MOBA_Q_BLOCK
        qc = lax.dynamic_slice_in_dim(q, q_start, MOBA_Q_BLOCK, axis=2)
        q_pos = q_start + jnp.arange(MOBA_Q_BLOCK)
        own = q_start // MOBA_BLOCK
        gate = jnp.einsum('bhqd,bhnd->bhqn', qc, k_mean).astype(jnp.float32)
        gate = jnp.where(jnp.arange(nb) < own, gate, NEG_INF)
        _, sel = lax.top_k(gate, topk)
        valid = jnp.arange(topk) < own
        k_sel = k_blocks[b_idx, h_idx, sel]
        v_sel = v_blocks[b_idx, h_idx, sel]
        k_pos_sel = sel[..., None] * MOBA_BLOCK + blk_pos
        s_sel = jnp.einsum('bhqd,bhqnkd->bhqnk', qc, k_sel).astype(jnp.float32) * scale
        s_sel = s_sel + bias_tab[h_idx[..., None], t5_bucket(q_pos[:, None, None] - k_pos_sel)]
        s_sel = jnp.where(valid[:, None], s_sel, NEG_INF)
        s_sel = s_sel.reshape(b, h, MOBA_Q_BLOCK, topk * MOBA_BLOCK)
        own_start = own * MOBA_BLOCK
        k_own = lax.dynamic_slice_in_dim(kp, own_start, MOBA_BLOCK, axis=2)
        v_own = lax.dynamic_slice_in_dim(vp, own_start, MOBA_BLOCK, axis=2)
        rel = q_pos[:, None] - (own_start + blk_pos)[None, :]
        s_own = jnp.einsum('bhqd,bhkd->bhqk', qc, k_own).astype(jnp.float32) * scale
        s_own = jnp.where(rel >= 0, s_own + bias_tab[:, t5_bucket(rel)], NEG_INF)
        p = jax.nn.softmax(jnp.concatenate([s_sel, s_own], axis=-1), axis=-1).astype(v.dtype)
        p_sel = p[..., :topk * MOBA_BLOCK].reshape(b, h, MOBA_Q_BLOCK, topk, MOBA_BLOCK)
        p_own = p[..., topk * MOBA_BLOCK:]
        return (jnp.einsum('bhqnk,bhqnkd->bhqd', p_sel, v_sel)
                + jnp.einsum('bhqk,bhkd->bhqd', p_own, v_own))

    outs = lax.map(chunk, jnp.arange(s // MOBA_Q_BLOCK))
    return outs.transpose(1, 2, 0, 3, 4).reshape(b, h, s, dh)

def causal_block_attention(q, k, v, scale, decay=None):
    b, h, s, _ = q.shape
    dv = v.shape[-1]
    k_pos = jnp.arange(s)

    def chunk(c):
        q_start = c * Q_BLOCK
        qc = lax.dynamic_slice_in_dim(q, q_start, Q_BLOCK, axis=2)
        q_pos = q_start + jnp.arange(Q_BLOCK)
        sc = jnp.einsum('bhqd,bhkd->bhqk', qc, k).astype(jnp.float32) * scale
        if decay is not None:
            dq = lax.dynamic_slice_in_dim(decay, q_start, Q_BLOCK, axis=2)
            sc = sc + dq[..., None] - decay[:, :, None, :]
        sc = jnp.where(k_pos[None, :] <= q_pos[:, None], sc, NEG_INF)
        p = jax.nn.softmax(sc, axis=-1).astype(v.dtype)
        return jnp.einsum('bhqk,bhkd->bhqd', p, v)

    outs = lax.map(chunk, jnp.arange(s // Q_BLOCK))
    return outs.transpose(1, 2, 0, 3, 4).reshape(b, h, s, dv)

def hybrid_mixer(h, rel_bias, w_in, b_f, q_norm, kv_norm, w_uq, w_ukv, w_o):
    b, s, _ = h.shape
    pos = jnp.arange(s)
    proj = h @ w_in
    (a_q, a_k, a_v, c_q, c_kv, k_r, f_q, f_k, f_v, f_g) = jnp.split(
        proj, np.cumsum(PROJ_SIZES)[:-1].tolist(), axis=-1)

    out_a = moba_attention(split_heads(a_q, N_HEADS_MOBA, HEAD_DIM),
                           split_heads(a_k, N_HEADS_MOBA, HEAD_DIM),
                           split_heads(a_v, N_HEADS_MOBA, HEAD_DIM), rel_bias)

    qb = split_heads(rms_norm_2(c_q, q_norm) @ w_uq, N_HEADS_MLA, MLA_QK_DIM)
    kv = split_heads(rms_norm_2(c_kv, kv_norm) @ w_ukv, N_HEADS_MLA, MLA_NOPE_DIM + MLA_V_DIM)
    k_nope, v_b = kv[..., :MLA_NOPE_DIM], kv[..., MLA_NOPE_DIM:]
    q_b = jnp.concatenate([qb[..., :MLA_NOPE_DIM], rotary(qb[..., MLA_NOPE_DIM:], pos)], axis=-1)
    k_rope = jnp.broadcast_to(rotary(k_r[:, None], pos), (b, N_HEADS_MLA, s, MLA_ROPE_DIM))
    k_b = jnp.concatenate([k_nope, k_rope], axis=-1)
    out_b = causal_block_attention(q_b, k_b, v_b, MLA_QK_DIM ** -0.5)

    log_f = jax.nn.log_sigmoid(f_g.astype(jnp.float32) + b_f.astype(jnp.float32))
    decay = jnp.cumsum(log_f, axis=1).transpose(0, 2, 1)
    out_c = causal_block_attention(split_heads(f_q, N_HEADS_FOX, HEAD_DIM),
                                   split_heads(f_k, N_HEADS_FOX, HEAD_DIM),
                                   split_heads(f_v, N_HEADS_FOX, HEAD_DIM),
                                   HEAD_DIM ** -0.5, decay)

    merged = jnp.concatenate([merge_heads(out_a), merge_heads(out_b), merge_heads(out_c)], axis=-1)
    return merged @ w_o

def conv_ffn(h, w_up, conv_w, conv_b, w_down):
    u = h @ w_up
    u = lax.conv_general_dilated(u, conv_w[:, None, :], window_strides=(1,),
                                 padding=[(CONV_WIDTH - 1, 0)],
                                 dimension_numbers=('NWC', 'WIO', 'NWC'),
                                 feature_group_count=u.shape[-1]) + conv_b
    g, val = jnp.split(u, 2, axis=-1)
    return (jax.nn.gelu(g, approximate=True) * val) @ w_down

def second_inputs(seed: int = 0) -> dict:
    key = jax.random.key(seed)
    ks = jax.random.split(key, 20)
    f32 = jnp.float32

    def nrm(k, shape, fan_in):
        return jax.random.normal(k, shape, f32) * (fan_in ** -0.5)

    def gain(k, shape):
        return 1.0 + 0.1 * jax.random.normal(k, shape, f32)

    L = DEPTH_2
    return {
        "x": jax.random.normal(ks[0], (BATCH, SEQ, D_MODEL), f32),
        "rel_bias": 0.5 * jax.random.normal(ks[1], (T5_BUCKETS, N_HEADS_MOBA), f32),
        "ln_mix_pre": gain(ks[2], (L, D_MODEL)),
        "ln_mix_post": gain(ks[3], (L, D_MODEL)),
        "ln_ffn_pre": gain(ks[4], (L, D_MODEL)),
        "ln_ffn_post": gain(ks[5], (L, D_MODEL)),
        "w_in": nrm(ks[6], (L, D_MODEL, PROJ_COLS), D_MODEL),
        "b_f": 2.0 + 0.5 * jax.random.normal(ks[7], (L, N_HEADS_FOX), f32),
        "q_norm": gain(ks[8], (L, MLA_Q_RANK)),
        "kv_norm": gain(ks[9], (L, MLA_KV_RANK)),
        "w_uq": nrm(ks[10], (L, MLA_Q_RANK, N_HEADS_MLA * MLA_QK_DIM), MLA_Q_RANK),
        "w_ukv": nrm(ks[11], (L, MLA_KV_RANK, N_HEADS_MLA * (MLA_NOPE_DIM + MLA_V_DIM)), MLA_KV_RANK),
        "w_o": nrm(ks[12], (L, MIX_WIDTH, D_MODEL), MIX_WIDTH),
        "w_up": nrm(ks[13], (L, D_MODEL, 2 * D_FF_2), D_MODEL),
        "conv_w": nrm(ks[14], (L, CONV_WIDTH, 2 * D_FF_2), CONV_WIDTH),
        "conv_b": 0.01 * jax.random.normal(ks[15], (L, 2 * D_FF_2), f32),
        "w_down": nrm(ks[16], (L, D_FF_2, D_MODEL), D_FF_2),
    }

def second_block(x, rel_bias, ln_mix_pre, ln_mix_post, ln_ffn_pre, ln_ffn_post, w_in, b_f,
              q_norm, kv_norm, w_uq, w_ukv, w_o, w_up, conv_w, conv_b, w_down):
    for l in range(DEPTH_2):
        h = rms_norm_2(x, ln_mix_pre[l])
        x = x + rms_norm_2(hybrid_mixer(h, rel_bias, w_in[l], b_f[l], q_norm[l], kv_norm[l],
                                      w_uq[l], w_ukv[l], w_o[l]), ln_mix_post[l])
        h = rms_norm_2(x, ln_ffn_pre[l])
        x = x + rms_norm_2(conv_ffn(h, w_up[l], conv_w[l], conv_b[l], w_down[l]), ln_ffn_post[l])
    return x


def setup_inputs(seed=0):
    out = dict(first_inputs(seed))
    for name, value in second_inputs(seed + 1).items():
        if name != "x":
            out[name + "_2"] = value
    return out


def reference(
    x, mem, mix_norm_g, pool_w, pool_scale, sb_w_qkv, sb_w_o, s5_a_re, s5_a_im, s5_log_dt,
    s5_b_re, s5_b_im, s5_c_re, s5_c_im, s5_d, s5_w_glu, xa_norm_g, mem_norm_g, xa_wq, xa_wkv,
    xa_wo, ffn_norm_g, ffn_w_up, ffn_conv_w, ffn_conv_b, ffn_w_down, final_norm_g, rel_bias_2,
    ln_mix_pre_2, ln_mix_post_2, ln_ffn_pre_2, ln_ffn_post_2, w_in_2, b_f_2, q_norm_2,
    kv_norm_2, w_uq_2, w_ukv_2, w_o_2, w_up_2, conv_w_2, conv_b_2, w_down_2,
):
    x = first_block(
        x, mem, mix_norm_g, pool_w, pool_scale, sb_w_qkv, sb_w_o, s5_a_re, s5_a_im, s5_log_dt,
        s5_b_re, s5_b_im, s5_c_re, s5_c_im, s5_d, s5_w_glu, xa_norm_g, mem_norm_g, xa_wq,
        xa_wkv, xa_wo, ffn_norm_g, ffn_w_up, ffn_conv_w, ffn_conv_b, ffn_w_down, final_norm_g,
    )
    return second_block(
        x, rel_bias_2, ln_mix_pre_2, ln_mix_post_2, ln_ffn_pre_2, ln_ffn_post_2, w_in_2, b_f_2,
        q_norm_2, kv_norm_2, w_uq_2, w_ukv_2, w_o_2, w_up_2, conv_w_2, conv_b_2, w_down_2,
    )


_drawn_inputs = setup_inputs


def setup_inputs(seed=0):
    import zlib

    import numpy as np

    out = dict(_drawn_inputs(seed))
    spreads = {}
    factors = {'s5_a_re': 64.0,
     's5_a_im': 2.756,
     's5_log_dt': 2.783,
     's5_b_re': 13.924,
     's5_b_im': 12.478,
     's5_c_re': 11.343,
     's5_c_im': 13.002,
     'xa_norm_g': 8.0,
     'mem_norm_g': 6.261,
     'conv_b_2': 4.804}
    for name, (base, spread) in spreads.items():
        noise = np.random.default_rng([zlib.crc32(name.encode()), seed]).standard_normal(out[name].shape)
        drawn = base * np.exp(spread * noise) if base else spread * noise
        out[name] = __import__('jax').numpy.asarray(drawn.astype(out[name].dtype))
    for name, factor in factors.items():
        out[name] = (out[name] * factor).astype(out[name].dtype)
    return out
```

```python
import math
from contextlib import ExitStack

import numpy as np

import concourse.bass as bass
from concourse import mybir

ALU = mybir.AluOpType
ACT = mybir.ActivationFunctionType
F32 = mybir.dt.float32
F32R = mybir.dt.float32r
I32 = mybir.dt.int32
BF16 = mybir.dt.bfloat16
AX = mybir.AxisListType.X

P = 128
T = 256
D = 1024
KT = D // P
F = 2816
FT = F // P
UW = 2048
RING = 3
EPS = 1e-6
NEG = -1e30
MAGIC = 12582912.0
TWO_PI_PARTS = (6.28125, 0.0019350051879882812, 3.019916050561733e-07)
RSQRT_SEED = 0x5F3759DF
POOL_WINDOWS = (2, 4, 8, 16)
CUT, CUT_LOOP, CUT_BUSY = 768, 1024, 512
BUSY = ("cross0", "stick1", "cross1")

XA_UNITS = 16
FFN_UNITS = FT + FT // 2
TURNS = (FT - 2) // 4
MIXERS = ("pool", "stick", "s5", "pool")
MIXER_UNITS = {"pool": 1, "stick": 16, "s5": 8, "hybrid": 17}
N_UNITS = sum(MIXER_UNITS[k] + XA_UNITS + FFN_UNITS for k in MIXERS) + 2 * (MIXER_UNITS["hybrid"] + FFN_UNITS)

PV = {}
_n = 0
for _name, _w in ([(f"mix{i}", KT) for i in range(4)] + [(f"xa{i}", KT) for i in range(4)]
                  + [(f"mem{i}", KT) for i in range(4)] + [(f"ffn{i}", KT) for i in range(4)]
                  + [("final", KT), ("scale0", KT), ("scale1", KT), ("s5_d", KT)]
                  + [(f"{k}{i}", KT) for i in range(2) for k in ("mpre", "mpost", "fpre", "fpost")]
                  + [(f"qn{i}", 2) for i in range(2)] + [(f"kvn{i}", 1) for i in range(2)]
                  + [(f"bf{i}", 1) for i in range(2)] + [(f"conv{i}", FT * 8) for i in range(6)]):
    PV[_name] = _n
    _n += _w
N_PV = _n


MLA_SCALE = 96 ** -0.5
N_CONST_DMAS = 2
N_LATE_DMAS = 4
S5_STEPS = 23 + 2
S5_RESULTS = (6, 9, 8, 13, 14)
EXTRA = (16 + 4 * 16, 16 + 7 * 16)
S5_NORM = 1 + 3 * MIXERS.index("s5") + 1


class Marks:

    def __init__(self):
        self.unit = 0
        self.part = 0
        self.evac = 0
        self.bank = [0] * RING
        self.xpair = 0
        self.sq = 0
        self.added = 0
        self.norm = 0
        self.head = 0
        self.o = 0
        self.tile = 0
        self.h = 0
        self.mix = 0
        self.split = 0

    def splits(self, u, n):
        todo = range(self.split, min(u + 1, n))
        self.split = max(self.split, todo.stop)
        return todo

    def took(self):
        self.bank[self.unit % RING] = self.evac + 1
        self.evac += 1
        self.unit += 1


class Group:

    def __init__(self, kind, first, n, par, o0, heads=None, bias=None, decay=None):
        self.kind, self.first, self.n, self.par, self.o0 = kind, first, n, par, o0
        self.heads = heads or [(kind, i) for i in range(n)]
        self.bias, self.decay = bias, decay
        self.outputs = n if kind == "xa" else n // 2


def early(l, hd, n):
    return MIXERS[l] == "pool" and hd == 0 and n < 2


def group_o(g, i):
    return g.o0 if g.kind == "xa" else g.o0 + i // 2


def ends(g, i):
    return g.kind == "xa" or i % 2 == 1


def done_o(g, i):
    return i if g.kind == "xa" else i // 2


def hybrid_groups(m):
    a = Group("heads", m.head, 4, 0, 0, [("moba", i) for i in range(4)], bias=(0, 1, 2, 3))
    b = Group("heads", m.head + 4, 8, 1, 2,
              [("mla", i) for i in range(4)] + [("moba", 0), ("moba", 1), ("fox", 2), ("fox", 3)],
              bias=(0, 0, 0, 0, 4, 5), decay=(0, 0, 0, 0, 0, 0, 4, 5))
    c = Group("heads", m.head + 12, 4, 0, 6, [("fox", i) for i in range(4)], decay=(0, 1, 2, 3))
    m.head += 16
    return a, b, c


def program(pool, stick, s5, cross, ffn, hybrid):
    out = []
    for l, kind in enumerate(MIXERS):
        out += [(f"{kind}{l}", {"pool": pool, "stick": stick, "s5": s5}[kind]), (f"cross{l}", cross), (f"ffn{l}", ffn)]
    for l in range(2):
        out += [(f"hybrid{l}", hybrid), (f"ffn{4 + l}", ffn)]
    return out


def share(u):
    names = [name for name, _ in program(*[None] * 6)]
    n = max(i for i in range(len(names)) if units_until(i) <= u)
    for i in (n - 1, n):
        if i >= 0 and names[i][:3] == "ffn" and 5 <= u - units_until(i) < 5 + 6 * TURNS:
            return CUT_LOOP
    return CUT_BUSY if names[n] in BUSY else CUT


def units_until(stop):
    n = {"pool": 1, "stick": 16, "s5": 8, "cross": XA_UNITS, "hybrid": 17, "ffn": FFN_UNITS}
    names = [name for name, _ in program(*[None] * 6)]
    return sum(n[name[:-1]] for name in names[:stop]) + (2 if stop and names[min(stop, len(names)) - 1][:4] == "pool" else 0)


def build_decoder(nc, w_all, x_t, mem_t, pv, consts, invcnt, rope, s5_p, s5_b, s5_c, moba_t, moba_oh, sel,
                  out, stop=99):
    ctx = ExitStack()
    with ctx:
        def sb(name, shape, dt=F32):
            return ctx.enter_context(nc.sbuf_tensor(name, shape, dt))

        def sem(name):
            return ctx.enter_context(nc.semaphore(name))

        raw = [sb(f"raw{i}", [P, UW]) for i in range(RING)]
        whi = [sb(f"whi{i}", [P, UW], F32R) for i in range(RING)]
        wlo = [sb(f"wlo{i}", [P, UW], F32R) for i in range(RING)]
        xhi, xlo = sb("xhi", [P, KT, T], F32R), sb("xlo", [P, KT, T], F32R)
        ohi, olo = sb("ohi", [P, KT, T], F32R), sb("olo", [P, KT, T], F32R)
        mhi, mlo = sb("mhi", [P, KT, T], F32R), sb("mlo", [P, KT, T], F32R)
        hhi, hlo = sb("hhi", [P, 4, T], F32R), sb("hlo", [P, 4, T], F32R)
        res = sb("res", [P, KT, T])
        sq = sb("sq", [P, KT, T])
        hn = sb("hn", [P, KT, T])
        par = sb("par", [P, N_PV])
        ident = sb("ident", [P, P])
        ones = sb("ones", [P, P])
        mask = sb("mask", [P, 3 * P])
        zero = sb("zero", [P, P], BF16)
        rb = sb("rb", [P, T])
        rbm = sb("rbm", [P, T])
        rbq = sb("rbq", [P, 2, T])
        rt = sb("rt", [P, 4])
        rtm = sb("rtm", [P, 4])
        nx = sb("nx", [P, 12])
        diag = sb("diag", [P, 4, P])
        small = sb("small", [P, 32])
        gw = sb("gw", [P, 5, 32])
        gtmp = sb("gtmp", [P, 2, 32 * 8])
        s5v = sb("s5v", [P, 5, 32])
        e1 = sb("e1", [P, 2, 32, 16])
        e16 = sb("e16", [P, 2, 32, 16])
        scr = sb("scr", [P, 7680])

        ybank = [ctx.enter_context(nc.psum_tensor(f"y{i}", [P, 2, T], F32)) for i in range(RING)]
        four = ctx.enter_context(nc.psum_tensor("four", [P, 4, 2, T], F32))
        abank = [four[:, i, :, :] for i in range(4)]
        stat = ctx.enter_context(nc.psum_tensor("stat", [P, 2, T], F32))
        sbank = [abank[0], abank[1]]
        tbank, obank = abank[2], abank[3]

        def flat(ap):
            return ap.rearrange("p a b -> p (a b)")

        q_sb = [scr[:, 512 * i:512 * i + 512].rearrange("p (a t) -> p a t", a=2) for i in range(2)]
        k_sb = [scr[:, 1024 + 512 * i:1536 + 512 * i].rearrange("p (a t) -> p a t", a=2) for i in range(2)]
        v_sb = [scr[:, 2048 + 512 * i:2560 + 512 * i].rearrange("p (a t) -> p a t", a=2) for i in range(2)]
        mla_q = scr[:, 3072:3584].rearrange("p (a t) -> p a t", a=2)
        mla_k = scr[:, 3584:4096].rearrange("p (a t) -> p a t", a=2)
        mla_v = scr[:, 4096:4608].rearrange("p (a t) -> p a t", a=2)
        mla_qr, mla_kr = scr[:, 4608:4864], scr[:, 4864:5120]
        p_sb = [scr[:, 5120 + 512 * i:5632 + 512 * i] for i in range(3)]
        pt_sb = [scr[:, 6656 + 512 * i:7168 + 512 * i] for i in range(2)]
        cq, ck, ks = (p_sb[i].rearrange("p (a t) -> p a t", a=2) for i in range(3))
        tmp = [pt_sb[0][:, 0:T], pt_sb[0][:, T:2 * T], pt_sb[1][:, 0:T], pt_sb[1][:, T:2 * T]]
        sel_sb = sq[:, 3:6, :].rearrange("p a t -> p (a t)").rearrange("p (h n) -> p h n", n=P)
        dec, negdec = sq[:, 6, :], sq[:, 7, :]
        moba_bias = hn[:, 0:6, :]
        cos_sb, sin_sb = hn[:, 6, :], hn[:, 7, :]
        u_sb = [scr[:, 516 * i:516 * i + 516].rearrange("p (a t) -> p a t", a=2) for i in range(2)]
        c_sb = [scr[:, 1032 + 512 * i:1544 + 512 * i].rearrange("p (a t) -> p a t", a=2) for i in range(2)]
        t_sb = [scr[:, 2056 + 256 * i:2312 + 256 * i] for i in range(2)]
        hf_sb = [scr[:, 2568 + 256 * i:2824 + 256 * i] for i in range(2)]
        pa = scr[:, 0:2176].rearrange("p (k t) -> p k t", k=KT)
        pb = scr[:, 2176:4352].rearrange("p (k t) -> p k t", k=KT)
        pinv = scr[:, 4352:5376].rearrange("p (g t) -> p g t", g=4)
        pm = scr[:, 5376:7424].rearrange("p (k t) -> p k t", k=KT)
        def s5(at):
            return scr[:, at:at + 512].rearrange("p (a t) -> p a t", a=2)
        rot = [scr[:, 1024 * i:1024 * i + 1024] for i in range(2)]
        tc_sb, ts_sb = [s5(0), s5(1024)], [s5(512), s5(1536)]
        ra, ia, p0, p1 = ([s5(1024 * n), s5(1024 * n + 512)] for n in range(2, 6))
        p2 = [sq[:, 4 + 2 * i:6 + 2 * i, :] for i in range(2)]
        table_sb = [scr[:, 4096 + 512 * i:4608 + 512 * i] for i in range(2)]
        bt = [scr[:, 6144 + 256 * i:6400 + 256 * i].rearrange("p (c s) -> p c s", c=2) for i in range(2)]
        ct = [scr[:, 6656 + 256 * i:6912 + 256 * i].rearrange("p (c j f) -> p c j f", c=2, j=4) for i in range(2)]
        cc = [scr[:, 7168:7552].rearrange("p (c j f) -> p c j f", c=3, j=4),
              diag[:].rearrange("p a n -> p (a n)")[:, 0:384].rearrange("p (c j f) -> p c j f", c=3, j=4)]
        g_sb = [sq[:, 0, :], sq[:, 1, :]]
        yu = sq[:, 2, :]
        ctmp = [sq[:, 3, 128 * i:128 * i + 128].rearrange("p (j f) -> p j f", j=4) for i in range(2)]
        omb, carry = scr[:, 3072:3456], scr[:, 3456:3842]
        cgate = [scr[:, 256 * i:256 * i + 256] for i in range(2)]
        cval = [scr[:, 512 + 256 * i:768 + 256 * i] for i in range(2)]

        def pc(name, i=0):
            return par[:, PV[name] + i:PV[name] + i + 1]

        raw_in = [sem(f"raw_in{i}") for i in range(RING)]
        consts_in = sem("consts_in")
        mem_in = sem("mem_in")
        extra_in = sem("extra_in")
        w_hi = sem("w_hi")
        w_lo_v = sem("w_lo_v")
        w_lo_p = sem("w_lo_p")
        unit_done = sem("unit_done")
        part_done = sem("part_done")
        evac = sem("evac")
        x_hi, x_lo = sem("x_hi"), sem("x_lo")
        m_hi, m_lo = sem("m_hi"), sem("m_lo")
        squared = sem("squared")
        added = sem("added")
        summed = sem("summed")
        diag_ok = sem("diag_ok")
        spread = sem("spread")
        rb_ok = sem("rb_ok")
        square_in = sem("square_in")
        x_in = sem("x_in")
        late_in = sem("late_in")
        mask_in = sem("mask_in")
        hn_ok = sem("hn_ok")
        scored = sem("scored")
        ready = sem("ready")
        exped = sem("exped")
        probs = sem("probs")
        turned = sem("turned")
        pt_ok = sem("pt_ok")
        valued = sem("valued")
        o_hi, o_lo = sem("o_hi"), sem("o_lo")
        mixed = sem("mixed")
        conv = sem("conv")
        gated = sem("gated")
        prod = sem("prod")
        h_hi, h_lo = sem("h_hi"), sem("h_lo")
        own_v = sem("own_v")
        own_g = sem("own_g")
        own_a = sem("own_a")
        moba_ps = sem("moba_ps")
        moba_sb = sem("moba_sb")
        moba_out = sem("moba_out")
        s5_a, s5_v, s5_t = sem("s5_a"), sem("s5_v"), sem("s5_t")
        s5_in = [sem(f"s5_in{i}") for i in range(2)]
        table = sem("table")
        table_out = [sem(f"table_out{i}") for i in range(2)]
        table_in = [sem(f"table_in{i}") for i in range(2)]
        cmat = sem("cmat")
        bu_ok = sem("bu_ok")
        bu_used = sem("bu_used")
        prods = sem("prods")
        prods_g = sem("prods_g")
        scanned = sem("scanned")
        y_ok = sem("y_ok")
        gelu_ok = sem("gelu_ok")
        sig_ok = sem("sig_ok")
        fg_ok, fa_ok, ln_ok = sem("fg_ok"), sem("fa_ok"), sem("ln_ok")
        zeroed = sem("zeroed")
        out_in = sem("out_in")
        finished = sem("finished")

        block = ctx.enter_context(nc.Block())
        n_units = max(2 * RING, units_until(stop))

        def s5p(n):
            return hn[0:32, n // 2, P * (n % 2):P * (n % 2) + P]

        moba_tab, moba_dist = scr[0:33, 3072:3840], scr[0:33, 3840:4224]
        moba_rows = [flat(hn)[:, 3 * P * i:3 * P * i + 3 * P] for i in range(5)] + [scr[:, 4224:4608]]

        scratch = nc.dram_tensor("moba_scratch", [6, P, 3 * P], F32, kind="Internal").ap()
        rotations = nc.dram_tensor("rotations", [16, P, 1024], F32, kind="Internal").ap()
        toeplitz = bass.AP(tensor=scratch.tensor, offset=P - 1,
                           ap=[[3 * P - 1, P], [3 * P * P, 6], [1, 2 * P]])

        def between_heads(g, slot, last, score, soften, turn, value):
            if g is None:
                return
            for lag, step in ((1, soften), (0, score), (2, turn), (3, value)):
                if step and 0 <= slot - lag < g.n:
                    step(g, slot - lag)
            if slot == last:
                for i in range(max(0, last - 2), g.n):
                    if step_left(last, 2, i) and turn:
                        turn(g, i)
                    if value:
                        value(g, i)

        def step_left(last, lag, i):
            return i > last - lag

        @block.tensor
        def _(pe):
            m = Marks()

            def start_unit(u, bank_free=None):
                pe.wait_ge(w_lo_v, u + 1)
                pe.wait_ge(w_lo_p, u + 1)
                if bank_free is not None:
                    pe.wait_ge(evac, bank_free)

            def free(s):
                return m.bank[s] or None

            def three(out_ap, s, cols, xh, xl, first, last):
                pe.matmul(out_ap, whi[s][:, cols], xh, start=first, stop=False, skip_group_check=True)
                pe.matmul(out_ap, whi[s][:, cols], xl, start=False, stop=False, skip_group_check=True)
                return pe.matmul(out_ap, wlo[s][:, cols], xh, start=False, stop=last, skip_group_check=True)

            def three_t(out_ap, s, cols, xh, xl, first, last):
                pe.matmul(out_ap, xh, whi[s][:, cols], start=first, stop=False, skip_group_check=True)
                pe.matmul(out_ap, xh, wlo[s][:, cols], start=False, stop=False, skip_group_check=True)
                return pe.matmul(out_ap, xl, whi[s][:, cols], start=False, stop=last, skip_group_check=True)

            def tiles(s, kt, xh, xl, by_token, first, last):
                for i in range(2):
                    if by_token:
                        cols, tok = slice(kt * 256, kt * 256 + 256), slice(i * P, i * P + P)
                        mm = three_t(ybank[s][:, i, :], s, cols, xh[:, kt, tok], xl[:, kt, tok],
                                     first and i == 0, last)
                    else:
                        cols = slice(kt * 256 + i * P, kt * 256 + i * P + P)
                        mm = three(ybank[s][:, i, :], s, cols, xh[:, kt, :], xl[:, kt, :],
                                   first and i == 0, last)
                return mm

            def project(src, by_token=False, fresh=None, per=2, between=None, nslots=2):
                u, s = m.unit, m.unit % RING
                xh, xl = {"x": (xhi, xlo), "o": (ohi, olo), "m": (mhi, mlo)}[src]
                start_unit(u, free(s))
                for kt in range(KT):
                    if fresh is not None and kt % per == 0:
                        pe.wait_ge(fresh[0], fresh[1] + kt // per + 1)
                    mm = tiles(s, kt, xh, xl, by_token, kt == 0, kt == KT - 1)
                    if kt == KT - 1:
                        mm.then_inc(unit_done, 1)
                    if between and (kt + 1) % (KT // nslots) == 0:
                        between((kt + 1) // (KT // nslots) - 1)
                m.took()

            def project_out(g):
                u0 = m.unit
                for j in range(3):
                    s = (u0 + j) % RING
                    start_unit(u0 + j, free(s))
                    if j == 0:
                        pe.wait_ge(o_lo, m.o)
                    for kt in range(6):
                        tiles(s, kt, ohi, olo, False, kt == 0, False)
                        if kt % 3 == 2:
                            attend(g, 2 * j + kt // 3, 5)
                pe.wait_ge(o_lo, m.o)
                for j in range(3):
                    s = (u0 + j) % RING
                    for kt in (6, 7):
                        mm = tiles(s, kt, ohi, olo, False, False, kt == 7)
                    mm.then_inc(unit_done, 1)
                    m.took()
                project("o")

            def sums(groups):
                for c, tls in enumerate(groups):
                    for tt in range(2):
                        for n, k in enumerate(tls):
                            mm = pe.matmul(stat[:, 0, 2 * c + tt:2 * c + tt + 1], sq[:, k, tt * P:tt * P + P],
                                           ones[:, 0:1], start=(n == 0), stop=(n == len(tls) - 1))
                mm.then_inc(summed, 1)

            def norm_sums():
                m.sq += 4
                m.added += 1
                pe.wait_ge(added, m.added)
                if m.norm:
                    pe.wait_ge(rb_ok, m.norm)
                sums([range(1)])

            def norm_spread(n=1):
                m.norm += 1
                pe.wait_ge(diag_ok, m.norm)
                for c in range(n):
                    for tt in range(2):
                        mm = pe.matmul(stat[:, c, tt * P:tt * P + P], ones[:], diag[:, 2 * c + tt, :],
                                       start=True, stop=True)
                mm.then_inc(spread, 1)

            def score(g, i):
                a = g.first + i
                kind, hd = g.heads[i]
                s = flat(sbank[a % 2])
                if i == 0:
                    pe.wait_ge(evac, g.out)
                if a >= 2:
                    pe.wait_ge(exped, a - 1)
                if kind == "xa":
                    for qt in range(2):
                        for dt in range(2):
                            mm = pe.matmul(s[:, qt * T:qt * T + T], q_sb[g.par][:, dt, qt * P:qt * P + P],
                                           k_sb[g.par][:, dt, :], start=(dt == 0), stop=(dt == 1))
                    mm.then_inc(scored, 1)
                    return
                po = 64 * (hd % 2)
                rows = slice(po, po + 64)
                qs, kk = (mla_q, mla_k) if kind == "mla" else (q_sb[g.par], k_sb[g.par])
                for qt in range(2):
                    o = s[:, 0:P] if qt == 0 else s[:, P:3 * P]
                    toks, keys = slice(qt * P, qt * P + P), slice(0, P + qt * P)
                    mm = pe.matmul(o, qs[rows, hd // 2, toks], kk[rows, hd // 2, keys],
                                   start=True, stop=kind not in ("mla", "fox"), skip_group_check=True)
                    if kind == "mla":
                        r = slice(po + 32 * (hd // 2), po + 32 * (hd // 2) + 32)
                        mm = pe.matmul(o, mla_qr[r, toks], mla_kr[r, keys], start=False, stop=True,
                                       skip_group_check=True)
                    if kind == "fox":
                        fh, r = g.decay[i], slice(po, po + 6)
                        for kt in range(qt + 1):
                            ok = s[:, (qt + kt) * P:(qt + kt) * P + P]
                            pe.matmul(ok, dec[r, toks], sel_sb[r, fh, :], start=False, stop=False,
                                      skip_group_check=True)
                            mm = pe.matmul(ok, sel_sb[r, fh, :], negdec[r, kt * P:kt * P + P], start=False,
                                           stop=True, skip_group_check=True)
                mm.then_inc(scored, 1)

            def turn(g, i):
                a = g.first + i
                pe.wait_ge(probs, a + 1)
                if a >= 1:
                    pe.wait_ge(pt_ok, a)
                pr, t = p_sb[a % 3], flat(tbank)
                if g.kind == "xa":
                    blocks = [(qt * T + kt * P, kt * T + qt * P) for qt in range(2) for kt in range(2)]
                else:
                    blocks = [(0, 0), (P, P), (2 * P, 2 * P)]
                for src, dst in blocks:
                    mm = pe.transpose(t[:, dst:dst + P], pr[:, src:src + P], ident[:])
                mm.then_inc(turned, 1)

            def value(g, i):
                a = g.first + i
                kind, hd = g.heads[i]
                pe.wait_ge(pt_ok, a + 1)
                n = m.o + done_o(g, i)
                if n:
                    pe.wait_ge(o_lo, n)
                pt = pt_sb[a % 2]
                if kind == "xa":
                    for dt in range(2):
                        for kt in range(2):
                            mm = pe.matmul(obank[:, dt, :], v_sb[g.par][:, kt, dt * P:dt * P + P],
                                           pt[:, kt * T:kt * T + T], start=(kt == 0), stop=(kt == 1))
                else:
                    po = 64 * (hd % 2)
                    vs, c = (mla_v if kind == "mla" else v_sb[g.par]), slice(hd * 64, hd * 64 + 64)
                    pe.matmul(obank[po:po + 64, 0, :], vs[:, 0, c], pt[:, 0:T], start=True, stop=False,
                              skip_group_check=True)
                    mm = pe.matmul(obank[po:po + 64, 0, P:T], vs[:, 1, c], pt[:, T:T + P], start=False,
                                   stop=True, skip_group_check=True)
                mm.then_inc(valued, 1)

            def attend(g, slot, last):
                between_heads(g, slot, last, score, None, turn, value)
                if g is not None and slot == last:
                    m.o += g.outputs

            def prepare(n):
                if n == 5:
                    pe.wait_ge(rb_ok, m.norm)
                    pe.wait_ge(s5_v, S5_STEPS)
                    for i, r in enumerate(S5_RESULTS):
                        mm = pe.transpose(stat[:, 0, i * 32:i * 32 + 32], s5p(r), ident[0:32, 0:32])
                    mm.then_inc(s5_t, 1)
                if 6 <= n < 12:
                    if n == 6:
                        pe.wait_ge(s5_v, S5_STEPS + 1)
                    else:
                        pe.wait_ge(moba_sb, n - 6)
                    pe.matmul(flat(stat)[:, 0:3 * P], moba_tab[:, (n - 6) * P:(n - 5) * P], moba_dist, start=True,
                              stop=True).then_inc(moba_ps, 1)

            def cross(l):
                pend = None
                for hd in range(4):
                    g = Group("xa", m.head, 1, hd % 2, 2 * hd)
                    for n, (src, tok) in enumerate((("m", False), ("m", True), ("x", False))):
                        if hd == 0 and n == 0:
                            pe.wait_ge(m_lo, l + 1)
                        late = MIXERS[l] == "pool"
                        if hd == 0 and n == 2 and not late:
                            norm_sums()
                        def between(c):
                            if late and c == 0 and (hd, n) == (0, 2):
                                norm_sums()
                            if late and c == 0 and (hd, n) == (1, 0):
                                norm_spread()
                            attend(pend, 2 * n + c, 5)
                        if not early(l, hd, n):
                            project(src, tok, fresh=(x_lo, m.xpair) if hd == 0 and n == 2 else None,
                                    between=between)
                        if hd == 0 and n == 2:
                            m.xpair += 4
                            if not late:
                                norm_spread()
                        if l == 0:
                            prepare(3 * hd + n)
                    m.head += 1
                    pend = g
                    g.out = m.evac
                project_out(pend)
                if l == 0:
                    pe.wait_ge(moba_sb, 6)

            def down(s, p):
                for b in range(4):
                    for mt in (2 * b, 2 * b + 1):
                        for kt in range(2):
                            c = kt * D + mt * P
                            mm = three(abank[b][:, mt % 2, :], s, slice(c, c + P), hhi[:, 2 * p + kt, :], hlo[:, 2 * p + kt, :],
                                       False, True)
                    yield b, mm

            def ffn():
                u0, e0, f0 = m.unit, m.evac, m.h
                project("x", fresh=(x_lo, m.xpair))
                m.xpair += 4
                norm_sums()
                project("x", between=lambda c: c or norm_spread())
                for b in range(4):
                    pe.matmul(flat(abank[b]), zero[:], zero[:, 0:1].to_broadcast([P, 2 * T]), start=True, stop=True)
                with nc.tensor.Fori(0, TURNS) as t:
                    for i in range(6):
                        u, j = u0 + 2 + i, 2 + i - i // 3
                        s = u % RING
                        if i % 3 < 2:
                            start_unit(t * 6 + u, t * 4 + (e0 + j - 1))
                            for kt in range(KT):
                                mm = tiles(s, kt, xhi, xlo, False, kt == 0, kt == KT - 1)
                        else:
                            start_unit(t * 6 + u)
                            pe.wait_ge(h_lo, t * 4 + (f0 + 2 * (i // 3) + 2))
                            for _, mm in down(s, i // 3):
                                pass
                        mm.then_inc(unit_done, 1)
                start_unit(u0 + FFN_UNITS - 1)
                pe.wait_ge(h_lo, f0 + FT)
                for b, mm in down((u0 + FFN_UNITS - 1) % RING, 0):
                    mm.then_inc(part_done if b < 3 else unit_done, 1)
                m.unit, m.h, m.evac = u0 + FFN_UNITS, f0 + FT, e0 + FT + 4
                m.bank = [m.evac] * RING

            def pool(l):
                norm_sums()
                norm_spread()
                pe.wait_ge(m_lo, l + 1)
                project("m")
                project("m", True)
                u, s = m.unit, m.unit % RING
                start_unit(u)
                for g in range(4):
                    pe.wait_ge(o_lo, m.o + g + 1)
                    for i in range(2):
                        for kt in range(2):
                            c = (2 * g + kt) * 256 + i * P
                            mm = three(abank[g][:, i, :], s, slice(c, c + P), ohi[:, 2 * g + kt, :],
                                       olo[:, 2 * g + kt, :], kt == 0 and i == 0, kt == 1)
                    mm.then_inc(unit_done if g == 3 else part_done, 1)
                m.o += 4
                m.unit += 1
                m.evac += 4

            def stick():
                pend = None
                for gi in range(4):
                    g = Group("stick", m.head, 4, gi % 2, 2 * gi)
                    for n in range(3):
                        project("x", n == 2, fresh=(x_lo, m.xpair) if gi == 0 and n == 0 else None,
                                between=(lambda c, n=n: attend(pend, 2 * n + c, 5)))
                        if gi == 0 and n == 0:
                            norm_sums()
                        if gi == 0 and n == 1:
                            norm_spread()
                    m.head += 4
                    pend = g
                    g.out = m.evac
                m.xpair += 4
                project_out(pend)

            def s5_layer():
                norm_sums()
                norm_spread()
                pe.wait_ge(hn_ok, 1)
                pe.wait_ge(evac, m.evac)
                for hf in range(17):
                    if hf < 16:
                        ft, half = hf // 2, hf % 2
                        if half == 0:
                            pe.wait_ge(s5_in[ft % 2], 32 * (ft // 2 + 1))
                        if hf >= 2:
                            pe.wait_ge(bu_used, hf - 1)
                        for jj in range(2):
                            r = slice(64 * half + 32 * jj, 64 * half + 32 * jj + 32)
                            for c in range(2):
                                mm = pe.matmul(abank[2 * half + jj][:, c, :], bt[ft % 2][r, c, :], hn[r, ft, :],
                                               start=True, stop=True)
                        mm.then_inc(bu_ok, 1)
                    if hf >= 1:
                        ft, half = (hf - 1) // 2, (hf - 1) % 2
                        if half == 0:
                            pe.wait_ge(cmat, ft + 1)
                            if ft >= 2:
                                pe.wait_ge(evac, m.evac + ft - 1)
                        for n, (arr, c) in enumerate(((p0, 0), (ra, 2), (p1, 1), (p2, 2))):
                            pe.wait_ge(prods if n < 2 else prods_g, 2 * (hf - 1) + n % 2 + 1)
                            for jj in range(2):
                                j = 2 * half + jj
                                mm = pe.matmul(ybank[ft % 2][32 * j:32 * j + 32, 0, :], cc[ft % 2][:, c, j, :],
                                               arr[half][:, jj, :], start=(n == 0), stop=(n == 3))
                        mm.then_inc(y_ok, 1)
                m.evac += 8
                m.bank = [m.evac] * RING
                project("o", fresh=(o_lo, m.o), per=1)
                m.o += 8
                for n in range(7):
                    project("o")

            def hybrid(l):
                for n in range(3):
                    project("x", fresh=(x_lo, m.xpair) if n == 0 else None)
                    if n == 0:
                        norm_sums()
                    if n == 1:
                        norm_spread()
                for n in range(3):
                    project("x", n == 2)
                    if n == 0:
                        m.sq += 1
                        pe.wait_ge(squared, m.sq)
                        pe.wait_ge(rb_ok, m.norm)
                        sums([range(0, 2), range(2, 3)])
                    if n == 1:
                        norm_spread(2)
                ga, gm, gc = hybrid_groups(m)
                u, s = m.unit, m.unit % RING
                start_unit(u)
                pe.wait_ge(h_lo, m.h + 1)
                for b, c0, kts, by_token in ((0, 0, (0, 1), False), (1, 512, (0, 1), False), (2, 1024, (2,), False),
                                             (3, 1280, (2,), True)):
                    for n, kt in enumerate(kts):
                        c, last = c0 + 256 * n, n == len(kts) - 1
                        for i in range(2):
                            tk = slice(i * P, i * P + P)
                            if by_token:
                                mm = three_t(abank[b][:, i, :], s, slice(c, c + 256), hhi[:, kt, tk],
                                             hlo[:, kt, tk], n == 0 and i == 0, last)
                            else:
                                mm = three(abank[b][:, i, :], s, slice(c + i * P, c + i * P + P),
                                           hhi[:, kt, :], hlo[:, kt, :], n == 0 and i == 0, last)
                mm.then_inc(unit_done, 1)
                m.unit += 1
                m.h += 1
                m.evac += 1
                ga.out = m.evac
                for n in range(3):
                    project("x", n == 2, between=(lambda c, n=n: attend(ga, 2 * n + c, 5)))
                gm.out = m.evac
                pe.wait_ge(ln_ok, l + 1)
                for n in range(3):
                    project("x", n == 2, between=(lambda c, n=n: attend(gm, 4 * n + c, 11)), nslots=4)
                gc.out = m.evac
                m.xpair += 4
                project_out(gc)
                norm_sums()
                norm_spread()
                m.evac += 4

            pe.wait_ge(square_in, 32)
            norm_sums()
            norm_spread()
            for st, (name, fn) in enumerate(program(pool, stick, s5_layer, cross, ffn, hybrid)):
                if st == stop:
                    break
                fn(int(name[-1])) if name[:-1] in ("pool", "cross", "hybrid") else fn()
                if name in ("ffn3", "ffn4", "ffn5"):
                    norm_sums()
                    norm_spread()
                    m.evac += 4

        @block.scalar
        def _(act):
            m = Marks()
            own = [0]

            def settle(ins):
                own[0] += 1
                ins.then_inc(own_a, 1)
                act.wait_ge(own_a, own[0])

            def hi(u):
                for v in m.splits(u, n_units):
                    act.wait_ge(raw_in[v % RING], 16 * (v // RING + 1))
                    if v >= RING:
                        act.wait_ge(unit_done, v - (RING - 1))
                    act.activation(whi[v % RING][:], raw[v % RING][:], ACT.Copy).then_inc(w_hi, 1)

            def hi_loop(t, u):
                act.wait_ge(raw_in[u % RING], t * 32 + 16 * (u // RING + 1))
                act.wait_ge(unit_done, t * 6 + (u - (RING - 1)))
                act.activation(whi[u % RING][:], raw[u % RING][:], ACT.Copy).then_inc(w_hi, 1)

            def squares(src, j):
                act.activation(sq[:, 2 * j:2 * j + 2, :], src[:, 2 * j:2 * j + 2, :], ACT.Square)\
                   .then_inc(squared, 1)

            def inputs(j, gain):
                for k in (2 * j, 2 * j + 1):
                    ins = act.activation(xhi[:, k, :], res[:, k, :], ACT.Identity, scale=pc(gain, k), bias=0.0)
                ins.then_inc(x_hi, 1)

            def pair(j, gain, src=None):
                act.wait_ge(evac, m.evac + j + 1)
                if gain:
                    inputs(j, gain)
                squares(src if src is not None else res, j)

            def norm(dst=None, n=1):
                m.norm += 1
                act.wait_ge(spread, m.norm)
                act.activation(rb[:] if dst is None else dst, stat[:, 0, :] if n == 1 else stat[:], ACT.Copy)\
                   .then_inc(rb_ok, 1)

            def memory(l):
                act.wait_ge(mem_in, 16 * (l + 1))
                for k in range(KT):
                    ins = act.activation(mhi[:, k, :], hn[:, k, :], ACT.Identity, scale=pc(f"mem{l}", k), bias=0.0)
                ins.then_inc(m_hi, 1)

            def score(g, i):
                a = g.first + i
                kind, _ = g.heads[i]
                pr, c = p_sb[a % 3], 8 * (a % 3)
                act.wait_ge(ready, a + 1)
                if kind == "stick":
                    act.activation(pr[:, 0:3 * P], pr[:, 0:3 * P], ACT.Tanh, scale=0.5).then_inc(exped, 1)
                    return
                for qt in range(2):
                    if kind == "xa":
                        src, dst, sc = flat(sbank[a % 2])[:, qt * T:qt * T + T], pr[:, qt * T:qt * T + T], 1 / 16
                    else:
                        src = dst = pr[:, 0:P] if qt == 0 else pr[:, P:3 * P]
                        sc = 1.0
                    ins = act.activation(dst, src, ACT.Exp, bias=small[:, c + qt:c + qt + 1], scale=sc,
                                         accum_out=small[:, c + 2 + qt:c + 3 + qt])
                ins.then_inc(exped, 1)

            def turn(g, i):
                a = g.first + i
                act.wait_ge(turned, a + 1)
                if a >= 2:
                    act.wait_ge(valued, a - 1)
                w = 2 * T if g.kind == "xa" else 3 * P
                act.activation(pt_sb[a % 2][:, 0:w], flat(tbank)[:, 0:w], ACT.Copy,
                               scale=0.5 if g.kind == "stick" else 1.0).then_inc(pt_ok, 1)

            def value(g, i):
                if not ends(g, i):
                    return
                act.wait_ge(valued, g.first + i + 1)
                k = group_o(g, i)
                if g.kind == "xa":
                    act.activation(ohi[:, k:k + 2, :], obank[:], ACT.Copy).then_inc(o_hi, 1)
                else:
                    act.activation(ohi[:, k, :], obank[:, 0, :], ACT.Copy).then_inc(o_hi, 1)

            def attend(g, slot, last):
                between_heads(g, slot, last, score, None, turn, value)
                if g is not None and slot == last:
                    m.o += g.outputs

            def project_out(g, after):
                u0 = m.unit
                hi(u0 + 2)
                for slot in range(6):
                    attend(g, slot, 5)
                hi(u0 + 3)
                after(0)
                after(1)
                hi(u0 + 4)
                after(2)
                hi(u0 + 5)
                after(3)
                m.unit += 4
                m.evac += 4

            def advance(n=1):
                for _ in range(n):
                    hi(m.unit + 2)
                    m.unit += 1
                    m.evac += 1

            def prepare(n):
                if n == 0:
                    act.wait_ge(m_lo, 1)
                    for dst, src in ((hn[0:32, 0:1, :].rearrange("p a t -> p (a t)"), s5_p[:, 0:256]),
                                     (hn[0:32, 1, 0:P], s5_p[:, 256:384]), (moba_tab, moba_t),
                                     (moba_dist, moba_oh)):
                        act.dma_start(dst, src).then_inc(late_in, 16)
                if n == 3:
                    act.wait_ge(late_in, 16 * N_LATE_DMAS)
                    act.activation(s5p(3), s5p(2), ACT.Exp).then_inc(s5_a, 1)
                    act.wait_ge(s5_v, 1)
                    act.activation(s5p(6), s5p(4), ACT.Exp).then_inc(s5_a, 1)
                    act.wait_ge(s5_v, 8)
                    act.activation(s5p(8), s5p(5), ACT.Sin)
                    act.activation(s5p(9), s5p(5), ACT.Sin, scale=0.5).then_inc(s5_a, 1)
                if 7 <= n < 13:
                    act.wait_ge(moba_ps, n - 6)
                    act.activation(moba_rows[n - 7], flat(stat)[:, 0:3 * P], ACT.Copy).then_inc(moba_sb, 1)
                if n == 12:
                    act.wait_ge(moba_sb, 6)
                    act.dma_start(scratch[0:5].rearrange("h p n -> p h n"),
                                  flat(hn)[:, 0:15 * P].rearrange("p (h n) -> p h n", h=5)).then_inc(moba_out, 16)
                    act.dma_start(scratch[5], moba_rows[5]).then_inc(moba_out, 16)

            def cross(l):
                pend = None
                for hd in range(4):
                    g = Group("xa", m.head, 1, hd % 2, 2 * hd)
                    for n in range(3):
                        if l == 0:
                            prepare(3 * hd + n)
                        if early(l, hd, n):
                            continue
                        hi(m.unit + 2)
                        attend(pend, 2 * n, 5)
                        attend(pend, 2 * n + 1, 5)
                        m.unit += 1
                        m.evac += 1
                    if hd == 0:
                        norm()
                    m.head += 1
                    pend = g
                if l == 0:
                    prepare(12)
                project_out(pend, lambda j: pair(j, f"ffn{l}"))

            def gate(j, fn, t=0):
                act.wait_ge(conv, t * 12 + 3 * (m.tile + j) + 3)
                act.activation(t_sb[j % 2], c_sb[j % 2][:, 1, :], fn).then_inc(gated, 1)

            def gated_hi(j, t=0):
                act.wait_ge(prod, t * 4 + (m.tile + j + 1))
                act.activation(hhi[:, j % 4, :], hf_sb[j % 2], ACT.Copy).then_inc(h_hi, 1)

            def ffn(st, last=None, gain=None, gelu=False):
                u0 = m.unit
                fn = ACT.Gelu_apprx_tanh if gelu else ACT.Silu
                if st == 0:
                    act.wait_ge(moba_out, 32)
                    act.dma_start(mask[:], consts[2]).then_inc(mask_in, 16)
                if st in (1, 2):
                    act.wait_ge(m_lo, st + 1)
                if st < 3:
                    act.dma_start(hn[:], mem_t).then_inc(mem_in, 16)
                if st == 2:
                    act.dma_start(pinv, invcnt).then_inc(extra_in, 16)
                hi(u0 + 2)
                hi(u0 + 3)
                norm()
                hi(u0 + 4)
                gate(0, fn)
                gate(1, fn)
                gated_hi(0)
                gated_hi(1)
                if st < 3:
                    memory(st + 1)
                def turn_(t, last=False):
                    for i in range(6):
                        j = 2 + i - i // 3
                        if i % 3 == 1:
                            gated_hi(j - 1, t)
                        if not (last and i > 3):
                            hi_loop(t, u0 + 5 + i)
                        if i % 3 < 2:
                            gate(j, fn, t)
                        if i % 3 == 1:
                            gated_hi(j, t)
                ends_stream = u0 + FFN_UNITS == n_units
                with nc.scalar.Fori(0, TURNS - ends_stream) as t:
                    turn_(t)
                if ends_stream:
                    turn_(TURNS - 1, last=True)
                m.split = u0 + FFN_UNITS + 2
                m.unit, m.tile = u0 + FFN_UNITS, m.tile + FT
                m.evac += FT

            def down_pairs(gain, src=None):
                for j in range(4):
                    pair(j, gain, src)
                m.evac += 4

            def pool(l):
                norm()
                if l == 0:
                    act.wait_ge(consts_in, 16 * N_CONST_DMAS)
                    memory(0)
                hi(m.unit + 2)
                for g in range(4):
                    act.wait_ge(mixed, m.mix + 1)
                    m.mix += 1
                    act.activation(ohi[:, 2 * g:2 * g + 2, :], pm[:, 2 * g:2 * g + 2, :], ACT.Copy)\
                       .then_inc(o_hi, 1)
                m.o += 4
                hi(m.unit + 4)
                m.unit += 3
                m.evac += 2

            def stick():
                pend = None
                for gi in range(4):
                    g = Group("stick", m.head, 4, gi % 2, 2 * gi)
                    for n in range(3):
                        hi(m.unit + 2)
                        attend(pend, 2 * n, 5)
                        attend(pend, 2 * n + 1, 5)
                        m.unit += 1
                        m.evac += 1
                        if gi == 0 and n == 1:
                            norm()
                    m.head += 4
                    pend = g
                project_out(pend, lambda j: pair(j, "xa1"))

            def s5_layer():
                def load_matrices(ft):
                    act.dma_start(bt[ft % 2], s5_b[ft]).then_inc(s5_in[ft % 2], 16)
                    act.dma_start(ct[ft % 2], s5_c[ft]).then_inc(s5_in[ft % 2], 16)
                def load_rotations(hf):
                    act.dma_start(rot[hf % 2], rotations[hf]).then_inc(table_in[hf % 2], 16)
                def gelu(ft):
                    act.wait_ge(evac, m.evac + ft + 1)
                    act.activation(g_sb[ft % 2], yu, ACT.Gelu_apprx_tanh).then_inc(gelu_ok, 1)
                    act.wait_ge(gelu_ok, ft + 1)
                    act.activation(ohi[:, ft, :], g_sb[ft % 2], ACT.Copy).then_inc(o_hi, 1)
                act.wait_ge(summed, m.norm + 1)
                for i in range(2):
                    act.wait_ge(table_out[i], 16 * 16)
                load_rotations(0)
                load_matrices(0)
                load_rotations(1)
                load_matrices(1)
                norm()
                for hf in range(16):
                    if hf + 2 < 16:
                        act.wait_ge(prods, 2 * hf + 2)
                        act.wait_ge(prods_g, 2 * hf + 2)
                        load_rotations(hf + 2)
                    if hf % 2 and hf < 12:
                        act.wait_ge(cmat, hf // 2 + 1)
                        act.wait_ge(bu_ok, hf + 1)
                        load_matrices(hf // 2 + 2)
                    if hf >= 2 and hf % 2 == 0:
                        gelu(hf // 2 - 1)
                gelu(7)
                m.evac += 8
                m.o += 8
                for n in range(8):
                    hi(m.unit + 2)
                    act.wait_ge(unit_done, m.unit + 1)
                    act.activation(cgate[n % 2], ybank[m.unit % RING][:, 1, :], ACT.Sigmoid).then_inc(sig_ok, 1)
                    m.unit += 1
                    m.evac += 1
                    if n % 2:
                        act.wait_ge(evac, m.evac)
                        inputs(n // 2, "xa2")
                        squares(res, n // 2)

            def hybrid(l):
                if l == 0:
                    act.dma_start(mask[:], consts[3]).then_inc(extra_in, 16)
                act.wait_ge(moba_out, 32)
                act.dma_start(hn[:, 6:8, :], rope).then_inc(extra_in, 16)
                act.dma_start(moba_bias, toeplitz).then_inc(extra_in, 16)
                advance(1)
                act.wait_ge(summed, m.norm + 1)
                act.dma_start(sel_sb, sel).then_inc(extra_in, 16)
                advance(1)
                norm()
                act.wait_ge(evac, m.evac)
                act.activation(sq[:, 0:2, :], cq, ACT.Square)
                act.activation(sq[:, 2, :], ck[:, 0, :], ACT.Square).then_inc(squared, 1)
                for k in range(2):
                    act.activation(hhi[:, k, :], cq[:, k, :], ACT.Identity, scale=pc(f"qn{l}", k), bias=0.0)
                act.activation(hhi[:, 2, :], ck[:, 0, :], ACT.Identity, scale=pc(f"kvn{l}"), bias=0.0)\
                   .then_inc(h_hi, 1)
                advance(1)
                advance(2)
                norm(rbq[:], 2)
                act.wait_ge(fg_ok, l + 1)
                settle(act.activation(tmp[1], tmp[0], ACT.Abs))
                settle(act.activation(tmp[1], tmp[1], ACT.Exp, scale=-1.0))
                act.activation(tmp[1], tmp[1], ACT.Ln, bias=1.0).then_inc(fa_ok, 1)
                advance(1)
                ga, gm, gc = hybrid_groups(m)
                advance(1)
                m.h += 1
                for n in range(3):
                    hi(m.unit + 2)
                    attend(ga, 2 * n, 5)
                    attend(ga, 2 * n + 1, 5)
                    m.unit += 1
                    m.evac += 1
                for n in range(3):
                    hi(m.unit + 2)
                    for c in range(4):
                        attend(gm, 4 * n + c, 11)
                    m.unit += 1
                    m.evac += 1
                project_out(gc, lambda j: pair(j, None, hn))
                norm()
                down_pairs(f"fpre{l}")

            act.dma_start(ident[:], consts[0][:, 0:P]).then_inc(square_in, 16)
            act.dma_start(ones[:], consts[1][:, 0:P]).then_inc(square_in, 16)
            act.dma_start(hn[:], mem_t).then_inc(mem_in, 16)
            act.dma_start(res[:], x_t).then_inc(x_in, 16)
            for dst, src in ((par[:], pv), (pinv, invcnt)):
                act.dma_start(dst, src).then_inc(consts_in, 16)
            act.wait_ge(mem_in, 16)
            for j in range(4):
                squares(hn, j)
            act.wait_ge(x_in, 16)
            act.wait_ge(summed, 1)
            for j in range(4):
                squares(res, j)
            norm(rbm[:])
            hi(0)
            for st, (name, fn) in enumerate(program(pool, stick, s5_layer, cross, ffn, hybrid)):
                if st == stop:
                    break
                kind, l = name[:-1], int(name[-1])
                if kind == "ffn":
                    ffn(l, gelu=l >= 4)
                    if l < 3:
                        down_pairs({0: "mix1", 1: None, 2: None}[l])
                    elif l == 3:
                        down_pairs(None)
                        norm()
                        down_pairs("mpre0")
                    else:
                        down_pairs(None, hn)
                        norm()
                        if l == 4:
                            down_pairs("mpre1")
                elif kind == "cross":
                    cross(l)
                elif kind == "hybrid":
                    hybrid(l)
                else:
                    fn(l) if kind == "pool" else fn()
                    if kind == "pool":
                        down_pairs(f"xa{l}")

        @block.gpsimd
        def _(pool_):
            m = Marks()
            own = [0]
            steps = [0]

            def settle(ins):
                own[0] += 1
                ins.then_inc(own_g, 1)
                pool_.wait_ge(own_g, own[0])

            def lo(u):
                for v in m.splits(u, n_units):
                    pool_.wait_ge(w_hi, v + 1)
                    c = slice(0, share(v))
                    pool_.tensor_tensor(wlo[v % RING][:, c], raw[v % RING][:, c],
                                        whi[v % RING][:, c].bitcast(F32), ALU.subtract).then_inc(w_lo_p, 1)

            def lo_loop(t, u):
                pool_.wait_ge(w_hi, t * 6 + (u + 1))
                pool_.tensor_tensor(wlo[u % RING][:, 0:CUT_LOOP], raw[u % RING][:, 0:CUT_LOOP],
                                    whi[u % RING][:, 0:CUT_LOOP].bitcast(F32), ALU.subtract).then_inc(w_lo_p, 1)

            def power_step():
                n = steps[0]
                steps[0] += 1
                tab, k = (e1, n) if n < 4 else (e16, n - 4)
                w = 1 << k
                lo_, up = slice(0, w), slice(w, 2 * w)
                shape = [P, 32, w]
                wre = gw[:, 0, :].unsqueeze(2).to_broadcast(shape)
                wim = gw[:, 1, :].unsqueeze(2).to_broadcast(shape)
                t0 = gtmp[:, 0, 0:32 * w].rearrange("p (j n) -> p j n", n=w)
                t1 = gtmp[:, 1, 0:32 * w].rearrange("p (j n) -> p j n", n=w)
                ar, ai = tab[:, 0, :, lo_], tab[:, 1, :, lo_]
                settle(pool_.tensor_tensor(t0, ar, wre, ALU.mult))
                settle(pool_.tensor_tensor(t1, ai, wim, ALU.mult))
                settle(pool_.tensor_tensor(tab[:, 0, :, up], t0, t1, ALU.subtract))
                settle(pool_.tensor_tensor(t0, ar, wim, ALU.mult))
                settle(pool_.tensor_tensor(t1, ai, wre, ALU.mult))
                settle(pool_.tensor_tensor(tab[:, 1, :, up], t0, t1, ALU.add))
                settle(pool_.tensor_tensor(gw[:, 2, :], gw[:, 0, :], gw[:, 0, :], ALU.mult))
                settle(pool_.tensor_tensor(gw[:, 3, :], gw[:, 1, :], gw[:, 1, :], ALU.mult))
                settle(pool_.tensor_tensor(gw[:, 4, :], gw[:, 0, :], gw[:, 1, :], ALU.mult))
                settle(pool_.tensor_tensor(gw[:, 0, :], gw[:, 2, :], gw[:, 3, :], ALU.subtract))
                settle(pool_.tensor_tensor(gw[:, 1, :], gw[:, 4, :], gw[:, 4, :], ALU.add))

            def units(n, each=None):
                for i in range(n):
                    lo(m.unit + 2)
                    m.unit += 1
                    if each:
                        each(i)

            def ffn(st):
                u0 = m.unit
                lo(u0 + 4)
                ends_stream = u0 + FFN_UNITS == n_units
                with nc.gpsimd.Fori(0, TURNS - ends_stream) as t:
                    for i in range(6):
                        lo_loop(t, u0 + 5 + i)
                if ends_stream:
                    for i in range(4):
                        lo_loop(TURNS - 1, u0 + 5 + i)
                m.split = u0 + FFN_UNITS + 2
                m.unit = u0 + FFN_UNITS

            def table_part(n):
                hf, c = n // 2, n % 2
                js = slice(2 * hf, 2 * hf + 2)
                shape = [P, 2, 16, 16]
                ca, sa = (e16[:, i, js, :].unsqueeze(3).to_broadcast(shape) for i in range(2))
                cb, sb_ = (e1[:, i, js, :].unsqueeze(2).to_broadcast(shape) for i in range(2))
                if n >= 2:
                    pool_.wait_ge(table_out[n % 2], 16 * (n // 2))
                t = table_sb[n % 2].rearrange("p (j a b) -> p j a b", j=2, a=16)
                u = gtmp[:].rearrange("p c n -> p (c n)").rearrange("p (j a b) -> p j a b", j=2, a=16)
                settle(pool_.tensor_tensor(t, ca if c == 0 else sa, cb, ALU.mult))
                settle(pool_.tensor_tensor(u, sa if c == 0 else ca, sb_, ALU.mult))
                pool_.tensor_tensor(t, t, u, ALU.subtract if c == 0 else ALU.add).then_inc(table, 1)

            def s5_layer():
                pool_.wait_ge(summed, S5_NORM)
                for hf in range(17):
                    if hf:
                        g = (hf - 1) % 2
                        pool_.wait_ge(scanned, 2 * hf - 1)
                        pool_.tensor_tensor(p1[g], ts_sb[g], ia[g], ALU.mult).then_inc(prods_g, 1)
                        pool_.tensor_tensor(p2[g], tc_sb[g], ia[g], ALU.mult).then_inc(prods_g, 1)
                    if hf == 16:
                        break
                    ft, half = hf // 2, hf % 2
                    if half == 0:
                        pool_.wait_ge(s5_in[ft % 2], 32 * (ft // 2 + 1))
                        if ft:
                            pool_.wait_ge(cmat, ft)
                        if ft >= 2:
                            pool_.wait_ge(y_ok, 2 * ft - 2)
                        jf = slice(4 * ft, 4 * ft + 4)
                        fr, fi = (s5v[:, c, jf].unsqueeze(2).to_broadcast([P, 4, 32]) for c in (3, 4))
                        cr, ci = ct[ft % 2][:, 0], ct[ft % 2][:, 1]
                        o = cc[ft % 2]
                        settle(pool_.tensor_tensor(ctmp[0], cr, fr, ALU.mult))
                        settle(pool_.tensor_tensor(ctmp[1], ci, fi, ALU.mult))
                        settle(pool_.tensor_tensor(o[:, 0], ctmp[0], ctmp[1], ALU.subtract))
                        settle(pool_.tensor_tensor(o[:, 1], ctmp[1], ctmp[0], ALU.subtract))
                        settle(pool_.tensor_tensor(ctmp[0], cr, fi, ALU.mult))
                        settle(pool_.tensor_tensor(ctmp[1], ci, fr, ALU.mult))
                        settle(pool_.tensor_tensor(ctmp[0], ctmp[0], ctmp[1], ALU.add))
                        pool_.tensor_scalar(o[:, 2], ctmp[0], -1.0, None, ALU.mult).then_inc(cmat, 1)
                units(8)

            pool_.memset(zero[:], 0.0).then_inc(zeroed, 1)
            for tab in (e1, e16):
                settle(pool_.memset(tab[:, 0, :, 0:1], 1.0))
                settle(pool_.memset(tab[:, 1, :, 0:1], 0.0))
            lo(0)
            for st, (name, fn) in enumerate(program(None, None, None, None, None, None)):
                if st == stop:
                    break
                kind, l = name[:-1], int(name[-1])
                if kind == "ffn":
                    ffn(l)
                elif kind == "s5":
                    s5_layer()
                elif name == "cross0":
                    units(5)
                    pool_.wait_ge(s5_v, S5_STEPS + 1)
                    settle(pool_.tensor_copy(gw[:, 0:2, :], s5v[:, 1:3, :]))
                    units(9, lambda i: power_step() if i < 8 else None)
                elif kind == "stick":
                    pool_.wait_ge(moba_out, 32)
                    units(16, table_part)
                elif name == "cross1":
                    units(16, lambda i: table_part(16 + i))
                else:
                    units({"pool": 3, "cross": 14 if l < 4 and MIXERS[l] == "pool" else 16, "hybrid": 17}[kind])
        @block.vector
        def _(dve):
            m = Marks()
            own = [0]

            def step(ins):
                own[0] += 1
                ins.then_inc(own_v, 1)

            def settle(ins=None):
                if ins is not None:
                    step(ins)
                dve.wait_ge(own_v, own[0])

            def tt(out_, a, b, op):
                return dve.tensor_tensor(out_, a, b, op)

            def stt(out_, a, s, b, op0, op1):
                return dve.scalar_tensor_tensor(out_, a, s, b, op0, op1)

            def twice(ap):
                return ap.unsqueeze(1).to_broadcast([P, 2, T])

            def lo(u):
                for v in m.splits(u, n_units):
                    dve.wait_ge(w_hi, v + 1)
                    c = slice(share(v), UW)
                    tt(wlo[v % RING][:, c], raw[v % RING][:, c], whi[v % RING][:, c].bitcast(F32),
                       ALU.subtract).then_inc(w_lo_v, 1)

            def lo_loop(t, u):
                dve.wait_ge(w_hi, t * 6 + (u + 1))
                tt(wlo[u % RING][:, CUT_LOOP:], raw[u % RING][:, CUT_LOOP:], whi[u % RING][:, CUT_LOOP:].bitcast(F32),
                   ALU.subtract).then_inc(w_lo_v, 1)

            def norm(dst=None, means=((2, D),)):
                r = rt if dst is None else dst
                n = sum(c for c, _ in means)
                m.norm += 1
                dve.wait_ge(summed, m.norm)
                c0 = 0
                for c, width in means:
                    step(dve.tensor_scalar(nx[:, c0:c0 + c], stat[:, 0, c0:c0 + c], 1.0 / width, EPS,
                                           ALU.mult, ALU.add))
                    c0 += c
                settle()
                x, y, z = nx[:, 0:n], r[:, 0:n], nx[:, 4:4 + n]
                settle(dve.tensor_scalar(z.bitcast(I32), x.bitcast(I32), 1, None, ALU.logical_shift_right))
                settle(dve.tensor_scalar(y.bitcast(I32), z.bitcast(I32), -1, RSQRT_SEED, ALU.mult, ALU.add))
                for _ in range(3):
                    settle(stt(z, y, -0.5, y, ALU.mult, ALU.mult))
                    settle(tt(z, z, x, ALU.mult))
                    settle(stt(y, z, 1.5, y, ALU.add, ALU.mult))
                for c in range(n):
                    ins = dve.tensor_scalar(diag[:, c, :], ident[:], r[:, c:c + 1], None, ALU.mult)
                ins.then_inc(diag_ok, 1)

            def add_squares(j):
                dve.wait_ge(squared, m.sq + 1)
                m.sq += 1
                if j:
                    settle(tt(sq[:, 0:2, :], sq[:, 0:2, :], sq[:, 2 * j:2 * j + 2, :], ALU.add))
                if j == 3:
                    tt(sq[:, 0, :], sq[:, 0, :], sq[:, 1, :], ALU.add).then_inc(added, 1)

            def normed(dst, gain):
                dve.wait_ge(rb_ok, m.norm)
                for k in range(KT):
                    ins = stt(dst[:, k, :], res[:, k, :], pc(gain, k), rb[:], ALU.mult, ALU.mult)
                return ins

            def input_lo(j, gain):
                dve.wait_ge(x_hi, m.xpair + 1)
                m.xpair += 1
                for k in (2 * j, 2 * j + 1):
                    ins = stt(xlo[:, k, :], res[:, k, :], pc(gain, k), xhi[:, k, :].bitcast(F32),
                              ALU.mult, ALU.subtract)
                ins.then_inc(x_lo, 1)

            def memory(l):
                dve.wait_ge(m_hi, l + 1)
                for k in range(KT):
                    ins = stt(mlo[:, k, :], hn[:, k, :], pc(f"mem{l}", k), mhi[:, k, :].bitcast(F32),
                              ALU.mult, ALU.subtract)
                ins.then_inc(m_lo, 1)

            def score(g, i):
                a = g.first + i
                kind, _ = g.heads[i]
                s, pr, c = flat(sbank[a % 2]), p_sb[a % 3], 8 * (a % 3)
                dve.wait_ge(scored, a + 1)
                if a >= 3:
                    dve.wait_ge(turned, a - 2)
                if kind == "xa":
                    settle(dve.tensor_reduce(small[:, c:c + 2], sbank[a % 2][:], AX, ALU.max))
                    dve.tensor_scalar(small[:, c:c + 2], small[:, c:c + 2], -1 / 16, None, ALU.mult)\
                       .then_inc(ready, 1)
                    return
                if kind == "stick":
                    tt(pr[:, 0:3 * P], s[:, 0:3 * P], mask[:], ALU.add).then_inc(ready, 1)
                    return
                if kind == "moba":
                    b = moba_bias[:, g.bias[i], :]
                    step(tt(pr[:, 0:P], s[:, 0:P], b[:, P:T], ALU.add))
                    settle(tt(pr[:, P:3 * P], s[:, P:3 * P], b, ALU.add))
                else:
                    settle(stt(pr[:, 0:3 * P], s[:, 0:3 * P], MLA_SCALE if kind == "mla" else 1.0, mask[:],
                               ALU.mult, ALU.add))
                step(dve.tensor_reduce(small[:, c:c + 1], pr[:, 0:P], AX, ALU.max))
                settle(dve.tensor_reduce(small[:, c + 1:c + 2], pr[:, P:3 * P], AX, ALU.max))
                dve.tensor_scalar(small[:, c:c + 2], small[:, c:c + 2], -1.0, None, ALU.mult).then_inc(ready, 1)

            def soften(g, i):
                a = g.first + i
                pr, c = p_sb[a % 3], 8 * (a % 3)
                dve.wait_ge(exped, a + 1)
                if g.kind == "stick":
                    settle(dve.tensor_scalar(omb, pr[:, 0:3 * P], -0.5, 0.5, ALU.mult, ALU.add))
                    step(dve.tensor_tensor_scan(carry[:, P - 1::-1], omb[:, P - 1::-1], omb[:, 0:P], 1.0,
                                                ALU.mult, ALU.bypass))
                    settle(dve.tensor_tensor_scan(carry[:, P + T:P:-1], omb[:, 3 * P - 1:P - 1:-1],
                                                  omb[:, P:3 * P], 1.0, ALU.mult, ALU.bypass))
                    stt(pr[:, 0:P], pr[:, 0:P], 1.0, carry[:, 1:P + 1], ALU.add, ALU.mult)
                    stt(pr[:, P:3 * P], pr[:, P:3 * P], 1.0, carry[:, P + 2:P + T + 2], ALU.add, ALU.mult)\
                        .then_inc(probs, 1)
                    return
                settle(dve.reciprocal(small[:, c + 4:c + 6], small[:, c + 2:c + 4]))
                w = T if g.kind == "xa" else P
                dve.tensor_scalar(pr[:, 0:w], pr[:, 0:w], small[:, c + 4:c + 5], None, ALU.mult)
                dve.tensor_scalar(pr[:, w:w + T], pr[:, w:w + T], small[:, c + 5:c + 6], None, ALU.mult)\
                   .then_inc(probs, 1)

            def value(g, i):
                if not ends(g, i):
                    return
                k = group_o(g, i)
                dve.wait_ge(o_hi, m.o + done_o(g, i) + 1)
                if g.kind == "xa":
                    tt(olo[:, k:k + 2, :], obank[:], ohi[:, k:k + 2, :].bitcast(F32), ALU.subtract).then_inc(o_lo, 1)
                else:
                    tt(olo[:, k, :], obank[:, 0, :], ohi[:, k, :].bitcast(F32), ALU.subtract).then_inc(o_lo, 1)

            def attend(g, slot, last):
                between_heads(g, slot, last, score, soften, None, value)
                if g is not None and slot == last:
                    m.o += g.outputs

            def take(kind, par, scale=None, factor=None):
                dst = {"q": q_sb, "k": k_sb, "v": v_sb}[kind][par]
                dve.wait_ge(unit_done, m.unit + 1)
                y = ybank[m.unit % RING]
                if kind == "v":
                    r = rt if factor is None else factor
                    for i in range(2):
                        ins = dve.tensor_scalar(dst[:, i, :], y[:, i, :], r[:, i:i + 1], None, ALU.mult)
                elif scale is None:
                    ins = tt(dst, y[:], twice(rb[:] if factor is None else factor), ALU.mult)
                else:
                    ins = stt(dst, y[:], scale, twice(rb[:]), ALU.mult, ALU.mult)
                ins.then_inc(evac, 1)
                m.unit += 1
                m.evac += 1

            def project_out(g, update, gain):
                u0 = m.unit
                lo(u0 + 2)
                for slot in range(6):
                    attend(g, slot, 5)
                lo(u0 + 3)
                for j in range(3):
                    dve.wait_ge(unit_done, u0 + j + 1)
                    update(j, ybank[(u0 + j) % RING])
                for j in range(4):
                    if j == 3:
                        dve.wait_ge(unit_done, u0 + 4)
                        update(3, ybank[u0 % RING])
                    if j == 1:
                        lo(u0 + 4)
                    if gain:
                        input_lo(j, gain)
                    if j:
                        add_squares(j - 1)
                add_squares(3)
                lo(u0 + 5)
                m.unit += 4
                m.evac += 4

            def add_pair(j, bank):
                tt(res[:, 2 * j:2 * j + 2, :], bank[:], res[:, 2 * j:2 * j + 2, :], ALU.add).then_inc(evac, 1)

            def copy_pair(j, bank):
                dve.tensor_copy(hn[:, 2 * j:2 * j + 2, :], bank[:]).then_inc(evac, 1)

            n5 = [0]
            def s5_step(ins):
                n5[0] += 1
                ins.then_inc(s5_v, 1)
                dve.wait_ge(s5_v, n5[0])

            def prepare(n):
                R = s5p
                if n == 3:
                    dve.wait_ge(s5_a, 1)
                    s5_step(tt(R(4), R(0), R(3), ALU.mult))
                    s5_step(tt(R(5), R(1), R(3), ALU.mult))
                    s5_step(dve.tensor_scalar(R(7), R(5), 1 / (2 * np.pi), MAGIC, ALU.mult, ALU.add))
                    s5_step(dve.tensor_scalar(R(7), R(7), -MAGIC, None, ALU.add))
                    for part in TWO_PI_PARTS:
                        s5_step(stt(R(5), R(7), -part, R(5), ALU.mult, ALU.add))
                    s5_step(dve.tensor_scalar(R(5), R(5), 3.1415925, -3.1415925, ALU.min, ALU.max))
                if n == 4:
                    dve.wait_ge(s5_a, 3)
                    s5_step(tt(R(9), R(9), R(9), ALU.mult))
                    s5_step(dve.tensor_scalar(R(9), R(9), -2.0, 1.0, ALU.mult, ALU.add))
                    s5_step(tt(R(10), R(6), R(9), ALU.mult))
                    s5_step(dve.tensor_scalar(R(10), R(10), -1.0, None, ALU.add))
                    s5_step(tt(R(11), R(6), R(8), ALU.mult))
                    s5_step(tt(R(12), R(0), R(0), ALU.mult))
                    s5_step(tt(R(13), R(1), R(1), ALU.mult))
                    s5_step(tt(R(12), R(12), R(13), ALU.add))
                    s5_step(dve.reciprocal(R(12), R(12)))
                    s5_step(tt(R(13), R(10), R(0), ALU.mult))
                    s5_step(tt(R(14), R(11), R(1), ALU.mult))
                    s5_step(tt(R(13), R(13), R(14), ALU.add))
                    s5_step(tt(R(13), R(13), R(12), ALU.mult))
                    s5_step(tt(R(14), R(11), R(0), ALU.mult))
                    s5_step(tt(R(15), R(10), R(1), ALU.mult))
                    s5_step(tt(R(14), R(14), R(15), ALU.subtract))
                    s5_step(tt(R(14), R(14), R(12), ALU.mult))
                    assert n5[0] == S5_STEPS, n5
                if n == 6:
                    dve.wait_ge(s5_t, 1)
                    s5_step(dve.tensor_copy(s5v[:].rearrange("p a b -> p (a b)"), stat[:, 0, 0:160]))

            def cross(l):
                pend = None
                for hd in range(4):
                    g = Group("xa", m.head, 1, hd % 2, 2 * hd)
                    for n, kind in enumerate("kvq"):
                        if l == 0:
                            prepare(3 * hd + n)
                        if early(l, hd, n):
                            continue
                        lo(m.unit + 2)
                        attend(pend, 2 * n, 5)
                        if n == 0 and g.first >= 2:
                            dve.wait_ge(valued, g.first - 1)
                        if hd == 0 and n == 2:
                            norm()
                            dve.wait_ge(rb_ok, m.norm)
                        take(kind, g.par, factor={"k": rbm[:], "v": rtm[:], "q": None}[kind])
                        attend(pend, 2 * n + 1, 5)
                    m.head += 1
                    pend = g
                project_out(pend, add_pair, f"ffn{l}")

            def take_tile(j, u, t=0):
                dve.wait_ge(unit_done, t * 6 + (u + 1))
                tt(u_sb[j % 2][:, :, 2:T + 2], ybank[u % RING][:], twice(rb[:]), ALU.mult).then_inc(evac, 1)

            def convolve(j, l, e0, t=None):
                f = m.tile + j
                t4, t12 = (t * 4, t * 12) if t is not None else (0, 0)
                us, cs = u_sb[j % 2], c_sb[j % 2]
                def w(i, k):
                    c = PV[f"conv{l}"] + 8 * j + 4 * i + k
                    if t is None:
                        return par[:, c:c + 1]
                    return par[:, bass.ds(t * 32 + c, 1)]
                dve.wait_ge(evac, t4 + (e0 + j + 1))
                dve.tensor_scalar(cs[:, 0, :], us[:, 0, 2:T + 2], w(0, 2), w(0, 3), ALU.mult, ALU.add)
                dve.tensor_scalar(cs[:, 1, :], us[:, 1, 2:T + 2], w(1, 2), w(1, 3), ALU.mult, ALU.add)\
                   .then_inc(conv, 1)
                for k in (1, 0):
                    dve.wait_ge(conv, t12 + (3 * f + 2 - k))
                    for i in range(2):
                        ins = stt(cs[:, i, :], us[:, i, k:k + T],
                                  w(i, k), cs[:, i, :], ALU.mult, ALU.add)
                    ins.then_inc(conv, 1)

            def gate(j, t=0):
                dve.wait_ge(gated, t * 4 + (m.tile + j + 1))
                tt(hf_sb[j % 2], t_sb[j % 2], c_sb[j % 2][:, 0, :], ALU.mult).then_inc(prod, 1)

            def gated_lo(j, t=0):
                dve.wait_ge(h_hi, t * 4 + (m.h + j + 1))
                tt(hlo[:, j % 4, :], hf_sb[j % 2], hhi[:, j % 4, :].bitcast(F32), ALU.subtract).then_inc(h_lo, 1)

            def ffn(l):
                u0, e0 = m.unit, m.evac
                for i in range(2):
                    step(dve.memset(u_sb[i][:, :, 0:2], 0.0))
                settle()
                lo(u0 + 2)
                norm()
                lo(u0 + 3)
                dve.wait_ge(rb_ok, m.norm)
                take_tile(0, u0)
                take_tile(1, u0 + 1)
                convolve(0, l, e0)
                convolve(1, l, e0)
                gate(0)
                gate(1)
                lo(u0 + 4)
                gated_lo(0)
                gated_lo(1)
                def turn_(t, last=False):
                    for i in range(6):
                        j = 2 + i - i // 3
                        if i % 3 == 0:
                            take_tile(j, u0 + 2 + i, t)
                            convolve(j, l, e0, t)
                        if i % 3 == 1:
                            gate(j - 1, t)
                            take_tile(j, u0 + 2 + i, t)
                            convolve(j, l, e0, t)
                            gated_lo(j - 1, t)
                            gate(j, t)
                            gated_lo(j, t)
                        if not (last and i > 3):
                            lo_loop(t, u0 + 5 + i)
                ends_stream = u0 + FFN_UNITS == n_units
                with nc.vector.Fori(0, TURNS - ends_stream) as t:
                    turn_(t)
                if ends_stream:
                    turn_(TURNS - 1, last=True)
                m.split = u0 + FFN_UNITS + 2
                m.unit, m.tile, m.h, m.evac = u0 + FFN_UNITS, m.tile + FT, m.h + FT, e0 + FT

            def banks_out(update, gain):
                for j in range(4):
                    if j < 3:
                        dve.wait_ge(part_done, m.part + j + 1)
                    else:
                        dve.wait_ge(unit_done, m.unit)
                    update(j, abank[j])
                    if gain and j:
                        input_lo(j - 1, gain)
                    if j:
                        add_squares(j - 1)
                if gain:
                    input_lo(3, gain)
                add_squares(3)
                m.part += 3
                m.evac += 4

            def pool(l):
                norm()
                if l == 0:
                    lo(0)
                    dve.wait_ge(consts_in, 16 * N_CONST_DMAS)
                memory(l)
                lo(m.unit + 1)
                settle(normed(sq, f"mix{l}"))
                if l:
                    dve.wait_ge(extra_in, 16)
                src, dst = sq, pb
                for n, w in enumerate(POOL_WINDOWS):
                    ks, sh = slice(2 * n, KT), w // 2
                    step(tt(dst[:, ks, sh:T], src[:, ks, sh:T], src[:, ks, 0:T - sh], ALU.add))
                    settle(dve.tensor_copy(dst[:, ks, 0:sh], src[:, ks, 0:sh]))
                    src, dst = dst, (pa if n % 2 == 0 else pb)
                lo(m.unit + 2)
                for n in range(4):
                    k = slice(2 * n, 2 * n + 2)
                    s = pb if n % 2 == 0 else pa
                    settle(tt(pm[:, k, :], s[:, k, 0:T], twice(pinv[:, n, :]), ALU.mult))
                    tt(pm[:, k, :], pm[:, k, :], sq[:, k, :], ALU.subtract).then_inc(mixed, 1)
                for n in range(4):
                    k = slice(2 * n, 2 * n + 2)
                    dve.wait_ge(o_hi, m.o + n + 1)
                    tt(olo[:, k, :], pm[:, k, :], ohi[:, k, :].bitcast(F32), ALU.subtract).then_inc(o_lo, 1)
                m.o += 4
                take("k", 0, factor=rbm[:])
                take("v", 0, factor=rtm)
                lo(m.unit + 2)
                m.unit += 1
                def scaled(j, bank):
                    for i in range(2):
                        k = 2 * j + i
                        ins = stt(res[:, k, :], bank[:, i, :], pc(f"scale{l // 3}", k), res[:, k, :],
                                  ALU.mult, ALU.add)
                    ins.then_inc(evac, 1)
                banks_out(scaled, f"xa{l}")

            def stick():
                pend = None
                dve.wait_ge(mask_in, 16)
                step(dve.memset(carry[:, P:P + 1], 1.0))
                step(dve.memset(carry[:, P + T + 1:P + T + 2], 1.0))
                for gi in range(4):
                    g = Group("stick", m.head, 4, gi % 2, 2 * gi)
                    for n, kind in enumerate("qkv"):
                        lo(m.unit + 2)
                        if gi == 0 and n == 0:
                            norm()
                            lo(m.unit + 3)
                            dve.wait_ge(rb_ok, m.norm)
                            take(kind, g.par, scale=0.125)
                            continue
                        if gi == 0 and n == 1:
                            take(kind, g.par)
                            memory(1)
                            continue
                        attend(pend, 2 * n, 5)
                        if n == 0 and gi >= 2:
                            dve.wait_ge(valued, g.first - 4)
                        take(kind, g.par, scale=0.125 if kind == "q" else None)
                        attend(pend, 2 * n + 1, 5)
                    m.head += 4
                    pend = g
                project_out(pend, add_pair, "xa1")

            def s5_layer():
                norm()
                memory(2)
                dve.wait_ge(m_lo, 3)
                normed(hn, "mix2").then_inc(hn_ok, 1)
                def out_tile(ft):
                    dve.wait_ge(y_ok, 2 * ft + 2)
                    if ft:
                        dve.wait_ge(gelu_ok, ft)
                    stt(yu, hn[:, ft, :], pc("s5_d", ft), ybank[ft % 2][:, 0, :], ALU.mult, ALU.add)\
                        .then_inc(evac, 1)
                def out_lo(ft):
                    dve.wait_ge(o_hi, m.o + ft + 1)
                    tt(olo[:, ft, :], g_sb[ft % 2], ohi[:, ft, :].bitcast(F32), ALU.subtract).then_inc(o_lo, 1)
                dve.wait_ge(hn_ok, 1)
                for hf in range(16):
                    half = hf % 2
                    dve.wait_ge(table_in[half], 16 * (hf // 2 + 1))
                    dve.wait_ge(bu_ok, hf + 1)
                    if hf >= 2:
                        dve.wait_ge(y_ok, hf - 1)
                    br, bi = (four[:, 2 * half:2 * half + 2, c, :] for c in range(2))
                    c, s, r, i_, a, b = (x[half] for x in (tc_sb, ts_sb, ra, ia, p0, p1))
                    step(tt(a, c, br, ALU.mult))
                    settle(tt(b, s, bi, ALU.mult))
                    settle(tt(r, a, b, ALU.add))
                    step(tt(a, c, bi, ALU.mult))
                    ins = tt(b, s, br, ALU.mult)
                    ins.then_inc(bu_used, 1)
                    dve.wait_ge(bu_used, hf + 1)
                    settle(tt(i_, a, b, ALU.subtract))
                    for x in (i_, r):
                        for jj in range(2):
                            j = 2 * hf + jj
                            ins = dve.tensor_tensor_scan(x[:, jj, :], s5v[:, 0, j:j + 1].to_broadcast([P, T]),
                                                         x[:, jj, :], 0.0, ALU.mult, ALU.add)
                        ins.then_inc(scanned, 1)
                    dve.wait_ge(scanned, 2 * hf + 2)
                    tt(a, c, r, ALU.mult).then_inc(prods, 1)
                    tt(r, s, r, ALU.mult).then_inc(prods, 1)
                    if half == 0 and hf >= 2:
                        out_tile(hf // 2 - 1)
                    if half == 1 and hf >= 3:
                        out_lo(hf // 2 - 1)
                out_tile(7)
                out_lo(7)
                m.evac += 8
                m.o += 8
                for n in range(8):
                    lo(m.unit + 2)
                    dve.wait_ge(sig_ok, n + 1)
                    settle(tt(cval[n % 2], ybank[m.unit % RING][:, 0, :], cgate[n % 2], ALU.mult))
                    tt(res[:, n, :], cval[n % 2], res[:, n, :], ALU.add).then_inc(evac, 1)
                    m.unit += 1
                    m.evac += 1
                    if n % 2 == 0 and n:
                        input_lo(n // 2 - 1, "xa2")
                        add_squares(n // 2 - 1)
                input_lo(3, "xa2")
                add_squares(3)

            def update_by_norm(gain, next_gain=None):
                norm()
                dve.wait_ge(rb_ok, m.norm)
                for j in range(4):
                    for k in (2 * j, 2 * j + 1):
                        step(stt(hn[:, k, :], hn[:, k, :], pc(gain, k), rb[:], ALU.mult, ALU.mult))
                    settle()
                    ks = slice(2 * j, 2 * j + 2)
                    tt(res[:, ks, :], res[:, ks, :], hn[:, ks, :], ALU.add).then_inc(evac, 1)
                    if next_gain and j:
                        input_lo(j - 1, next_gain)
                        add_squares(j - 1)
                if next_gain:
                    input_lo(3, next_gain)
                    add_squares(3)
                m.evac += 4

            def hybrid(l):
                def latent(dst):
                    dve.wait_ge(unit_done, m.unit + 1)
                    tt(dst, ybank[m.unit % RING][:], twice(rb[:]), ALU.mult).then_inc(evac, 1)
                    m.unit += 1
                    m.evac += 1
                lo(m.unit + 2)
                norm()
                lo(m.unit + 3)
                dve.wait_ge(rb_ok, m.norm)
                latent(cq)
                latent(ck)
                lo(m.unit + 2)
                latent(ks)
                dve.wait_ge(h_hi, m.h + 1)
                for k in range(2):
                    stt(hlo[:, k, :], cq[:, k, :], pc(f"qn{l}", k), hhi[:, k, :].bitcast(F32), ALU.mult, ALU.subtract)
                stt(hlo[:, 2, :], ck[:, 0, :], pc(f"kvn{l}"), hhi[:, 2, :].bitcast(F32), ALU.mult, ALU.subtract)\
                    .then_inc(h_lo, 1)
                dve.wait_ge(evac, m.evac)
                dve.tensor_scalar(tmp[0], ks[:, 1, :], pc(f"bf{l}"), None, ALU.add).then_inc(fg_ok, 1)
                dve.wait_ge(extra_in, EXTRA[l])
                step(tt(tmp[2], ck[:, 1, :], cos_sb, ALU.mult))
                settle(tt(tmp[3], ks[:, 0, :], sin_sb, ALU.mult))
                tt(mla_kr, tmp[2], tmp[3], ALU.add)
                lo(m.unit + 2)
                m.sq += 1
                norm(rtm, ((2, 256), (2, 128)))
                dve.wait_ge(unit_done, m.unit + 1)
                take("q", 0, scale=0.125)
                lo(m.unit + 2)
                take("k", 0)
                lo(m.unit + 2)
                take("v", 0)
                dve.wait_ge(fa_ok, l + 1)
                settle(stt(tmp[2], tmp[0], 0.0, tmp[1], ALU.min, ALU.subtract))
                settle(dve.tensor_tensor_scan(dec, tmp[2], tmp[2], 0.0, ALU.add, ALU.bypass))
                dve.tensor_scalar(negdec, dec, -1.0, None, ALU.mult).then_inc(ln_ok, 1)
                ga, gm, gc = hybrid_groups(m)
                lo(m.unit + 2)
                dve.wait_ge(rb_ok, m.norm)
                dve.wait_ge(unit_done, m.unit + 1)
                tt(mla_q, abank[0][:], twice(rbq[:, 0, :]), ALU.mult)
                step(tt(tmp[2], abank[1][:, 0, :], cos_sb, ALU.mult))
                settle(tt(tmp[3], abank[1][:, 1, :], sin_sb, ALU.mult))
                settle(tt(tmp[2], tmp[2], tmp[3], ALU.add))
                tt(mla_qr, tmp[2], rbq[:, 0, :], ALU.mult)
                tt(mla_k, abank[2][:], twice(rbq[:, 1, :]), ALU.mult)
                for i in range(2):
                    ins = dve.tensor_scalar(mla_v[:, i, :], abank[3][:, i, :], rtm[:, 2 + i:3 + i], None, ALU.mult)
                ins.then_inc(evac, 1)
                m.unit += 1
                m.h += 1
                m.evac += 1
                for n, kind in enumerate("qkv"):
                    lo(m.unit + 2)
                    attend(ga, 2 * n, 5)
                    take(kind, 1, scale=0.125 if kind == "q" else None)
                    attend(ga, 2 * n + 1, 5)
                for n, kind in enumerate("qkv"):
                    lo(m.unit + 2)
                    for c in range(3):
                        attend(gm, 4 * n + c, 11)
                    if n == 0:
                        dve.wait_ge(valued, gm.first)
                    take(kind, 0, scale=0.125 if kind == "q" else None)
                    attend(gm, 4 * n + 3, 11)
                project_out(gc, copy_pair, None)
                update_by_norm(f"mpost{l}", f"fpre{l}")

            dve.wait_ge(square_in, 32)
            for j in range(4):
                add_squares(j)
            norm(rtm)
            for j in range(4):
                add_squares(j)
            for st, (name, fn) in enumerate(program(pool, stick, s5_layer, cross, ffn, hybrid)):
                if st == stop:
                    break
                kind, l = name[:-1], int(name[-1])
                if kind == "ffn":
                    ffn(l)
                    if l < 3:
                        banks_out(add_pair, {0: "mix1", 1: None, 2: None}[l])
                    elif l == 3:
                        banks_out(add_pair, None)
                        norm()
                        dve.wait_ge(rb_ok, m.norm)
                        for j in range(4):
                            for k in (2 * j, 2 * j + 1):
                                ins = stt(res[:, k, :], res[:, k, :], pc("final", k), rb[:], ALU.mult, ALU.mult)
                            ins.then_inc(evac, 1)
                            if j:
                                dve.wait_ge(evac, m.evac + j)
                                input_lo(j - 1, "mpre0")
                                add_squares(j - 1)
                        dve.wait_ge(evac, m.evac + 4)
                        input_lo(3, "mpre0")
                        add_squares(3)
                        m.evac += 4
                    else:
                        banks_out(copy_pair, None)
                        update_by_norm(f"fpost{l - 4}", "mpre1" if l == 4 else None)
                elif kind in ("cross", "pool", "hybrid"):
                    fn(l)
                else:
                    fn()
            settle()
            dve.wait_ge(evac, m.evac)
            dve.tensor_copy(nx[:, 0:1], nx[:, 0:1]).then_inc(finished, 1)

        @block.sync
        def _(sp):
            def load(u, t=0):
                sp.wait_ge(w_lo_v, t * RING + (u - RING + 1))
                sp.wait_ge(w_lo_p, t * RING + (u - RING + 1))
                sp.dma_start(raw[u % RING][:], w_all[t * RING + u]).then_inc(raw_in[u % RING], 16)

            def load_loop(first, end):
                with nc.sync.Fori(0, (end - first) // RING) as t:
                    for b in range(RING):
                        load(first + b, t)

            sp.wait_ge(x_in, 16)
            for b in range(RING):
                sp.dma_start(raw[b][:], w_all[b]).then_inc(raw_in[b], 16)
            tables_at = units_until(3) + 6
            t0, t1 = tables_at // RING * RING, min(n_units, -(-(tables_at + 32) // RING) * RING)
            load_loop(RING, t0)
            for u in range(t0, t1):
                load(u)
                n = u - tables_at
                if 0 <= n < 32:
                    sp.wait_ge(table, n + 1)
                    sp.dma_start(rotations[n // 2][:, 512 * (n % 2):512 * (n % 2) + 512],
                                 table_sb[n % 2]).then_inc(table_out[n % 2], 16)
            load_loop(t1, n_units // RING * RING)
            for u in range(n_units // RING * RING, n_units):
                load(u)
            sp.wait_ge(finished, 1)
            sp.dma_start(out, res[:]).then_inc(out_in, 16)
            sp.wait_ge(out_in, 16)



def _columns(w, cols):
    return w[:, cols].reshape(KT, P, 256).transpose(1, 0, 2).reshape(P, UW)


def _halves(w, j, first, second):
    return _columns(w, np.r_[first + j * P:first + (j + 1) * P, second + j * P:second + (j + 1) * P])


def _run_of(w, c0, n):
    return [_columns(w, slice(c0 + 256 * i, c0 + 256 * i + 256)) for i in range(n)]


def _ffn_units(up, dn, value, gate):
    ups = [_halves(up, j, value, gate) for j in range(FT)]
    downs = [dn[256 * t:256 * t + 256].reshape(2, P, D).transpose(1, 0, 2).reshape(P, UW) for t in range(FT // 2)]
    out = ups[0:2]
    for t in range(FT // 2 - 1):
        out += [ups[2 * t + 2], ups[2 * t + 3], downs[t]]
    return out + [downs[-1]]


def _thirds(w, n, order="qkv", width=D):
    at = {"q": 0, "k": width, "v": 2 * width}
    return [_columns(w, slice(at[c] + 256 * i, at[c] + 256 * i + 256)) for i in range(n) for c in order]


def _hybrid_units(w, uq, ukv, wo):
    mq, mk, mv, cq, ckv, kr, fq, fk, fv, fg = np.cumsum([0, 384, 384, 384, 256, 128, 32, 384, 384, 384])
    r = np.arange
    swap = np.r_[16:32, 0:16]
    gate = np.zeros((D, P), w.dtype)
    gate[:, 0:6] = gate[:, 64:70] = w[:, fg:fg + 6]
    units = [_columns(w, r(cq, cq + 256)),
             _columns(w, np.r_[ckv:ckv + P, np.tile(kr + r(32), 4)]),
             _columns(np.concatenate([w[:, np.tile(kr + swap, 4)], gate], axis=1), slice(0, 256))]
    units += [_columns(w, r(c, c + 256)) for c in (mq, mk, mv)]
    up = np.zeros((P, UW), w.dtype)
    order = (0, 2, 1, 3)
    nope = np.concatenate([96 * h + r(64) for h in range(4)])
    rope = np.concatenate([96 * h + 64 + r(32) for h in order])
    ropes = np.concatenate([96 * h + 64 + swap for h in order])
    q = uq.reshape(2, P, 384)
    for kt in range(2):
        up[:, 256 * kt:256 * kt + 256] = q[kt][:, nope]
        up[:, 512 + 256 * kt:768 + 256 * kt] = q[kt][:, np.r_[rope, ropes]]
    up[:, 1024:1280] = ukv[:, np.concatenate([128 * h + r(64) for h in range(4)])]
    up[:, 1280:1536] = ukv[:, np.concatenate([128 * h + 64 + r(64) for h in range(4)])]
    units.append(up)
    units += [_columns(w, np.r_[a + 256:a + 384, b + 256:b + 384]) for a, b in ((mq, fq), (mk, fk), (mv, fv))]
    units += [_columns(w, r(c, c + 256)) for c in (fq, fk, fv)]
    rows = np.r_[0:256, 384:640, 256:384, 896:1024, 640:896]
    return units + _run_of(wo[rows], 0, 4)


def _by_partition(v):
    return v.reshape(-1, P).T


def _bucket(rel):
    n = np.maximum(rel, 0)
    large = 16 + (np.log(np.maximum(n, 1).astype(np.float32) / 16) / math.log(64.0) * 16).astype(np.int32)
    return np.where(n < 16, n, np.minimum(large, 31))


def lay_out(i):
    f32 = np.float32
    units, params = [], []
    for l, kind in enumerate(MIXERS):
        j = l // 3
        cross = []
        for h in range(4):
            c = slice(256 * h, 256 * h + 256)
            cross += [_columns(i["xa_wkv"][l], c), _columns(i["xa_wkv"][l][:, D:], c), _columns(i["xa_wq"][l], c)]
        if kind == "pool":
            units += cross[0:2]
            cross = cross[2:]
            units.append(i["pool_w"][j].reshape(4, 2, P, 256).transpose(2, 0, 1, 3).reshape(P, UW))
        elif kind == "stick":
            units += _thirds(i["sb_w_qkv"][j], 4) + _run_of(i["sb_w_o"][j], 0, 4)
        else:
            units += [_halves(i["s5_w_glu"][j], n, 0, D) for n in range(KT)]
        units += cross + _run_of(i["xa_wo"][l], 0, 4)
        units += _ffn_units(i["ffn_w_up"][l], i["ffn_w_down"][l], 0, F)
    for l in range(2):
        units += _hybrid_units(i["w_in_2"][l], i["w_uq_2"][l], i["w_ukv_2"][l], i["w_o_2"][l])
        units += _ffn_units(i["w_up_2"][l], i["w_down_2"][l], F, 0)
    assert len(units) == N_UNITS

    for name in ("mix_norm_g", "xa_norm_g", "mem_norm_g", "ffn_norm_g"):
        params += [_by_partition(v) for v in i[name]]
    params += [_by_partition(i["final_norm_g"])] + [_by_partition(v) for v in i["pool_scale"]]
    params += [_by_partition(i["s5_d"][0])]
    for l in range(2):
        params += [_by_partition(i[f"{n}_2"][l]) for n in ("ln_mix_pre", "ln_mix_post", "ln_ffn_pre", "ln_ffn_post")]
    params += [_by_partition(v) for v in i["q_norm_2"]] + [_by_partition(v) for v in i["kv_norm_2"]]
    for l in range(2):
        b = np.zeros((P, 1), f32)
        b[0:6, 0] = b[64:70, 0] = i["b_f_2"][l]
        params.append(b)
    for w, b, value, gate in ([(i["ffn_conv_w"][l], i["ffn_conv_b"][l], 0, 1) for l in range(4)]
                              + [(i["conv_w_2"][l], i["conv_b_2"][l], 1, 0) for l in range(2)]):
        taps = np.concatenate([w, b[None]]).reshape(4, 2, FT, P)[:, [value, gate]]
        params.append(taps.transpose(3, 2, 1, 0).reshape(P, FT * 8))
    pv = np.concatenate(params, axis=1)
    assert pv.shape[1] == N_PV

    q, k = np.arange(P)[:, None], np.arange(P)[None]
    none = np.zeros((P, P), f32)
    strict = np.where(k < q, 0, NEG).astype(f32)
    causal = np.where(k <= q, 0, NEG).astype(f32)
    consts = np.stack([np.concatenate(c, axis=1) for c in (
        (np.eye(P, dtype=f32), none, none), (np.ones((P, P), f32), none, none),
        (strict, none, strict), (causal, none, causal))])
    invcnt = np.stack([1 / np.minimum(np.arange(1, T + 1), w).astype(f32) for w in POOL_WINDOWS])
    invcnt = np.broadcast_to(invcnt.astype(f32), (P, 4, T))
    inv = (10000.0 ** (-np.arange(16, dtype=f32) / 16)).astype(f32)
    ang = np.arange(T, dtype=f32)[None] * inv[:, None]
    cos = np.tile(np.cos(ang), (8, 1))
    sin = np.tile(np.concatenate([-np.sin(ang), np.sin(ang)]), (4, 1))
    rope = np.stack([cos, sin], axis=1).astype(f32)

    s5_p = np.concatenate([i["s5_a_re"][0].reshape(32, P), i["s5_a_im"][0].reshape(32, P),
                           np.repeat(i["s5_log_dt"][0].reshape(32, 2), 64, axis=1)], axis=1)
    s5_b = np.zeros((8, 4, 2, 16, 2, 2, 64), f32)
    s5_c = np.zeros((8, 2, 64, 2, 4, 2, 16), f32)
    for c, (b, o) in enumerate((("s5_b_re", "s5_c_re"), ("s5_b_im", "s5_c_im"))):
        bb = i[b][0].reshape(8, 4, 2, 64, 16)
        oo = i[o][0].reshape(8, 4, 2, 16, 64)
        for g in range(2):
            s5_b[:, :, g, :, c, g, :] = bb[:, :, g].transpose(0, 1, 3, 2)
            s5_c[:, g, :, c, :, g, :] = oo[:, :, g].transpose(0, 3, 1, 2)
    dist = 255 - np.arange(3 * P)
    onehot = np.zeros((33, 3 * P), f32)
    onehot[_bucket(dist), np.arange(3 * P)] = dist >= 0
    onehot[32] = np.where(dist >= 0, 0, NEG)
    moba_t = np.concatenate([np.repeat(i["rel_bias_2"][:, :, None], P, axis=2), np.ones((1, 6, P), f32)])
    sel = np.zeros((P, 6, P), f32)
    for h in range(6):
        sel[h, h] = sel[64 + h, h] = 1
    return {
        "w_all": np.stack(units), "x_t": i["x"][0].T.reshape(KT, P, T).transpose(1, 0, 2),
        "mem_t": i["mem"][0].T.reshape(KT, P, T).transpose(1, 0, 2), "pv": pv, "consts": consts,
        "invcnt": invcnt, "rope": rope, "s5_p": s5_p, "s5_b": s5_b.reshape(8, P, 2, P),
        "s5_c": s5_c.reshape(8, P, 2, 4, 32), "moba_t": moba_t.reshape(33, 6 * P), "moba_oh": onehot, "sel": sel,
    }


def kernel(**inputs):
    import concourse.bacc as bacc
    from concourse.bass_utils import run_bass_kernel_spmd

    nc = bacc.Bacc("TRN2", target_bir_lowering=False, num_devices=1)
    arrays, args = {}, {}
    for name, a in lay_out({k: np.asarray(v) for k, v in inputs.items()}).items():
        a = np.ascontiguousarray(a)
        arrays[f"in_{name}"] = a
        args[name] = nc.dram_tensor(f"in_{name}", a.shape, mybir.dt.from_np(a.dtype), kind="ExternalInput").ap()
    out = nc.dram_tensor("out_0", (P, KT, T), F32, kind="ExternalOutput").ap()
    build_decoder(nc, out=out, **args)
    got = run_bass_kernel_spmd(nc, [arrays], core_ids=[0]).results[0]["out_0"]
    return np.ascontiguousarray(np.asarray(got).transpose(2, 1, 0).reshape(1, T, D))
```
